# Optimizing a Trainium2 kernel written in Bass

```python
import math
import jax, jax.numpy as jnp
from jax import lax
import numpy as np

D_MODEL = 1024
BATCH = 1
SEQ = 512
DEPTH = 1

CTX_LEN = 256
GRID_W = 64
MIX_WIDTH = 2 * D_MODEL
SSD_DINNER = MIX_WIDTH // 2
SSD_HEADDIM = 64
SSD_HEADS = SSD_DINNER // SSD_HEADDIM
SSD_GROUPS = 2
SSD_STATE = 64
SSD_CHUNK = 128
SSD_CONV_CH = SSD_DINNER + 2 * SSD_GROUPS * SSD_STATE
GDN_WIDTH = MIX_WIDTH - SSD_DINNER
GDN_HEADDIM = 128
GDN_HEADS = GDN_WIDTH // GDN_HEADDIM
GDN_CHUNK = 64
GDN_CONV_CH = 3 * GDN_WIDTH
CONV_K = 5
N_DIR = 2
D_FF = 4 * D_MODEL
EPS = 1e-6
IN_SIZES = (SSD_DINNER, SSD_CONV_CH, N_DIR * SSD_HEADS, GDN_CONV_CH, GDN_WIDTH, N_DIR * GDN_HEADS, N_DIR * GDN_HEADS)
IN_DIM = sum(IN_SIZES)


def rmsnorm(x, g):
    xf = x.astype(jnp.float32)
    y = xf * lax.rsqrt(jnp.mean(xf * xf, axis=-1, keepdims=True) + EPS)
    return y.astype(x.dtype) * g

def l2norm(x):
    xf = x.astype(jnp.float32)
    return (xf * lax.rsqrt(jnp.sum(xf * xf, axis=-1, keepdims=True) + EPS)).astype(x.dtype)

def modulate(h, shift, scale):
    return h * (1.0 + scale) + shift

def dwconv(x, w, b):
    y = lax.conv_general_dilated(x, w[:, None, :].astype(x.dtype), window_strides=(1,),
                                 padding=[(CONV_K // 2, CONV_K // 2)],
                                 dimension_numbers=('NWC', 'WIO', 'NWC'),
                                 feature_group_count=x.shape[-1])
    return y if b is None else y + b

def conv_rows(x, w, b):
    bsz, n, ch = x.shape
    rows = n // GRID_W
    return dwconv(x.reshape(bsz * rows, GRID_W, ch), w, b).reshape(bsz, n, ch)

def split_cols(p):
    parts, start = [], 0
    for size in IN_SIZES:
        parts.append(p[..., start:start + size])
        start += size
    return parts

def _ident(t):
    return t

def _flip(t):
    return jnp.flip(t, axis=1)

def ssd_scan(xh, dt, A, Bm, Cm, h0, return_y):
    bsz, n, H, P = xh.shape
    G, N = Bm.shape[2], Bm.shape[3]
    Q = SSD_CHUNK
    nc = n // Q
    rep = H // G
    x_c = xh.reshape(bsz, nc, Q, H, P)
    dt_c = dt.reshape(bsz, nc, Q, H)
    B_c = jnp.repeat(Bm, rep, axis=2).reshape(bsz, nc, Q, H, N)
    acum = jnp.cumsum(dt_c * A, axis=2)
    xdt = x_c * dt_c[..., None]
    states = jnp.einsum('bcqhn,bcqh,bcqhp->bchpn', B_c, jnp.exp(acum[:, :, -1:] - acum), xdt)
    chunk_decay = jnp.exp(acum[:, :, -1])

    def step(h, inp):
        s, d = inp
        h_next = h * d[:, :, None, None] + s
        return h_next, (h if return_y else None)

    h_final, h_prev = lax.scan(step, h0, (jnp.moveaxis(states, 1, 0), jnp.moveaxis(chunk_decay, 1, 0)))
    if not return_y:
        return None, h_final
    C_c = jnp.repeat(Cm, rep, axis=2).reshape(bsz, nc, Q, H, N)
    h_prev = jnp.moveaxis(h_prev, 0, 1)
    causal = jnp.tril(jnp.ones((Q, Q), bool))
    seg = acum[:, :, :, None, :] - acum[:, :, None, :, :]
    lmat = jnp.exp(jnp.where(causal[:, :, None], seg, -jnp.inf))
    scores = jnp.einsum('bcihn,bcjhn->bcijh', C_c, B_c) * lmat
    y = (jnp.einsum('bcijh,bcjhp->bcihp', scores, xdt)
         + jnp.einsum('bcihn,bchpn->bcihp', C_c, h_prev) * jnp.exp(acum)[..., None])
    return y.reshape(bsz, n, H, P), h_final

def gdn_scan(q, k, v, g, beta, S0, return_y):
    bsz, n, H, K = q.shape
    V = v.shape[-1]
    Q = GDN_CHUNK
    nc = n // Q

    def chunk(t):
        return jnp.swapaxes(t.reshape((bsz, nc, Q) + t.shape[2:]), 2, 3)

    qc, kc, vc = chunk(q), chunk(k), chunk(v)
    gcum = jnp.cumsum(chunk(g), axis=-1)
    bc = chunk(beta)[..., None]
    k_beta = kc * bc
    incl = jnp.tril(jnp.ones((Q, Q), bool))
    strict = jnp.tril(jnp.ones((Q, Q), bool), -1)
    decay = jnp.exp(jnp.where(incl, gcum[..., :, None] - gcum[..., None, :], -jnp.inf))
    kk = jnp.einsum('bchik,bchjk->bchij', k_beta, kc) * decay
    tmat = (jnp.eye(Q, dtype=jnp.float32) + jnp.where(strict, kk, 0.0)).astype(jnp.float32)
    rhs = jnp.concatenate([vc * bc, k_beta * jnp.exp(gcum)[..., None]], axis=-1).astype(jnp.float32)
    sol = lax.linalg.triangular_solve(tmat, rhs, left_side=True, lower=True, unit_diagonal=True)
    u, w = sol[..., :V], sol[..., V:]
    k_dec = kc * jnp.exp(gcum[..., -1:] - gcum)[..., None]
    chunk_decay = jnp.exp(gcum[..., -1])
    xs = [u, w, k_dec, chunk_decay]
    if return_y:
        q_dec = qc * jnp.exp(gcum)[..., None]
        qk = jnp.einsum('bchik,bchjk->bchij', qc, kc) * decay
        xs += [q_dec, qk]
    xs = tuple(jnp.moveaxis(t, 1, 0) for t in xs)

    def step(S, inp):
        u_i, w_i, kd_i, d_i = inp[:4]
        v_new = u_i - jnp.einsum('bhqk,bhkv->bhqv', w_i, S)
        S_next = S * d_i[..., None, None] + jnp.einsum('bhqk,bhqv->bhkv', kd_i, v_new)
        if not return_y:
            return S_next, None
        qd_i, qk_i = inp[4:]
        o = jnp.einsum('bhqk,bhkv->bhqv', qd_i, S) + jnp.einsum('bhij,bhjv->bhiv', qk_i, v_new)
        return S_next, o

    S_final, o = lax.scan(step, S0, xs)
    if not return_y:
        return None, S_final
    o = jnp.swapaxes(jnp.moveaxis(o, 0, 1), 2, 3).reshape(bsz, n, H, V)
    return o, S_final

def ssd_out_norm(y, z, g):
    bsz, n = y.shape[:2]
    v = (y.reshape(bsz, n, SSD_DINNER) * jax.nn.silu(z)).astype(jnp.float32)
    v = v.reshape(bsz, n, SSD_GROUPS, SSD_DINNER // SSD_GROUPS)
    v = v * lax.rsqrt(jnp.mean(v * v, axis=-1, keepdims=True) + EPS)
    return v.reshape(bsz, n, SSD_DINNER) * g

def gdn_out_norm(o, gate, g):
    bsz, n = o.shape[:2]
    return (rmsnorm(o, g) * jax.nn.silu(gate.reshape(bsz, n, GDN_HEADS, GDN_HEADDIM))).reshape(bsz, n, GDN_WIDTH)

def ssd_parts(xbc, dt):
    b_, l_ = xbc.shape[:2]
    xs, bm, cm = jnp.split(xbc, [SSD_DINNER, SSD_DINNER + SSD_GROUPS * SSD_STATE], axis=-1)
    return (xs.reshape(b_, l_, SSD_HEADS, SSD_HEADDIM),
            bm.reshape(b_, l_, SSD_GROUPS, SSD_STATE),
            cm.reshape(b_, l_, SSD_GROUPS, SSD_STATE),
            dt.reshape(b_, l_, N_DIR, SSD_HEADS).astype(jnp.float32))

def gdn_parts(qkv, a, beta):
    b_, l_ = qkv.shape[:2]
    q, k, v = jnp.split(qkv, 3, axis=-1)
    hs = (b_, l_, GDN_HEADS, GDN_HEADDIM)
    q = l2norm(q.reshape(hs)) * (GDN_HEADDIM ** -0.5)
    k = l2norm(k.reshape(hs))
    return (q, k, v.reshape(hs),
            a.reshape(b_, l_, N_DIR, GDN_HEADS).astype(jnp.float32),
            jax.nn.sigmoid(beta.reshape(b_, l_, N_DIR, GDN_HEADS).astype(jnp.float32)))

def token_mixers(p_lat, p_ctx, ssd_conv_w, ssd_conv_b, ssd_dt_bias, ssd_A_log, ssd_D, ssd_norm_g,
                 gdn_conv_w, gdn_dt_bias, gdn_A_log, gdn_norm_g, ctx_out):
    bsz = p_lat.shape[0]
    z_l, xbc_l, dt_l, qkv_l, gate_l, a_l, b_l = split_cols(p_lat)
    z_c, xbc_c, dt_c, qkv_c, gate_c, a_c, b_c = split_cols(p_ctx)
    xbc_l = jax.nn.silu(conv_rows(xbc_l, ssd_conv_w, ssd_conv_b))
    xbc_c = jax.nn.silu(dwconv(xbc_c, ssd_conv_w, ssd_conv_b))
    qkv_l = jax.nn.silu(conv_rows(qkv_l, gdn_conv_w, None))
    qkv_c = jax.nn.silu(dwconv(qkv_c, gdn_conv_w, None))
    xs_l, bm_l, cm_l, dt_l = ssd_parts(xbc_l, dt_l)
    xs_c, bm_c, cm_c, dt_c = ssd_parts(xbc_c, dt_c)
    q_l, k_l, v_l, a_l, be_l = gdn_parts(qkv_l, a_l, b_l)
    q_c, k_c, v_c, a_c, be_c = gdn_parts(qkv_c, a_c, b_c)

    ssd_l = xs_l * ssd_D[:, None]
    gdn_l = 0.0
    if ctx_out:
        ssd_c = xs_c * ssd_D[:, None]
        gdn_c = 0.0
    for d in range(N_DIR):
        o = _ident if d == 0 else _flip
        A = -jnp.exp(ssd_A_log[d].astype(jnp.float32))
        dtc = jax.nn.softplus(dt_c[:, :, d] + ssd_dt_bias[d])
        dtl = jax.nn.softplus(dt_l[:, :, d] + ssd_dt_bias[d])
        h0 = jnp.zeros((bsz, SSD_HEADS, SSD_HEADDIM, SSD_STATE), jnp.float32)
        yc, h_ctx = ssd_scan(o(xs_c), o(dtc), A, o(bm_c), o(cm_c), h0, ctx_out)
        yl, _ = ssd_scan(o(xs_l), o(dtl), A, o(bm_l), o(cm_l), h_ctx, True)
        ssd_l = ssd_l + o(yl)
        rate = jnp.exp(gdn_A_log[d].astype(jnp.float32))
        gc = -rate * jax.nn.softplus(a_c[:, :, d] + gdn_dt_bias[d])
        gl = -rate * jax.nn.softplus(a_l[:, :, d] + gdn_dt_bias[d])
        s0 = jnp.zeros((bsz, GDN_HEADS, GDN_HEADDIM, GDN_HEADDIM), jnp.float32)
        oc, s_ctx = gdn_scan(o(q_c), o(k_c), o(v_c), o(gc), o(be_c[:, :, d]), s0, ctx_out)
        ol, _ = gdn_scan(o(q_l), o(k_l), o(v_l), o(gl), o(be_l[:, :, d]), s_ctx, True)
        gdn_l = gdn_l + o(ol)
        if ctx_out:
            ssd_c = ssd_c + o(yc)
            gdn_c = gdn_c + o(oc)
    y_lat = jnp.concatenate([ssd_out_norm(ssd_l, z_l, ssd_norm_g),
                             gdn_out_norm(gdn_l, gate_l, gdn_norm_g)], axis=-1).astype(p_lat.dtype)
    if not ctx_out:
        return y_lat, None
    y_ctx = jnp.concatenate([ssd_out_norm(ssd_c, z_c, ssd_norm_g),
                             gdn_out_norm(gdn_c, gate_c, gdn_norm_g)], axis=-1).astype(p_ctx.dtype)
    return y_lat, y_ctx

def sq_relu_mlp(h, w1, w2):
    return jnp.square(jax.nn.relu(h @ w1)) @ w2

def first_inputs(seed: int = 0) -> dict:
    key = jax.random.key(seed)
    ks = jax.random.split(key, 24)
    f32 = jnp.float32

    def nrm(k, shape, scale):
        return jax.random.normal(k, shape, f32) * scale

    def gain(k, shape):
        return 1.0 + nrm(k, shape, 0.02)

    def dt_bias(k, shape):
        dt = jnp.exp(jax.random.uniform(k, shape, f32, math.log(1e-3), math.log(1e-1)))
        return dt + jnp.log(-jnp.expm1(-dt))

    def a_log(k, shape):
        return jnp.log(jax.random.uniform(k, shape, f32, 1.0, 16.0))

    return {
        'x': nrm(ks[0], (BATCH, SEQ, D_MODEL), 1.0),
        'c': nrm(ks[1], (BATCH, D_MODEL), 1.0),
        'ctx': nrm(ks[2], (BATCH, CTX_LEN, D_MODEL), 1.0),
        'c_ctx': nrm(ks[3], (D_MODEL,), 1.0),
        'w_mod': nrm(ks[4], (DEPTH, D_MODEL, 6 * D_MODEL), 0.5 * D_MODEL ** -0.5),
        'b_mod': nrm(ks[5], (DEPTH, 6 * D_MODEL), 0.01),
        'norm1_g': gain(ks[6], (DEPTH, D_MODEL)),
        'w_in': nrm(ks[7], (DEPTH, D_MODEL, IN_DIM), D_MODEL ** -0.5),
        'ssd_conv_w': nrm(ks[8], (DEPTH, CONV_K, SSD_CONV_CH), CONV_K ** -0.5),
        'ssd_conv_b': nrm(ks[9], (DEPTH, SSD_CONV_CH), 0.01),
        'ssd_dt_bias': dt_bias(ks[10], (DEPTH, N_DIR, SSD_HEADS)),
        'ssd_A_log': a_log(ks[11], (DEPTH, N_DIR, SSD_HEADS)),
        'ssd_D': gain(ks[12], (DEPTH, SSD_HEADS)),
        'ssd_norm_g': gain(ks[13], (DEPTH, SSD_DINNER)),
        'gdn_conv_w': nrm(ks[14], (DEPTH, CONV_K, GDN_CONV_CH), CONV_K ** -0.5),
        'gdn_dt_bias': dt_bias(ks[15], (DEPTH, N_DIR, GDN_HEADS)),
        'gdn_A_log': a_log(ks[16], (DEPTH, N_DIR, GDN_HEADS)),
        'gdn_norm_g': gain(ks[17], (DEPTH, GDN_HEADDIM)),
        'w_out': nrm(ks[18], (DEPTH, MIX_WIDTH, D_MODEL), MIX_WIDTH ** -0.5),
        'norm2_g': gain(ks[19], (DEPTH, D_MODEL)),
        'w_mlp1': nrm(ks[20], (DEPTH, D_MODEL, D_FF), D_MODEL ** -0.5),
        'w_mlp2': nrm(ks[21], (DEPTH, D_FF, D_MODEL), D_FF ** -0.5),
        'final_g': gain(ks[22], (D_MODEL,)),
    }

def first_block(x, c, ctx, c_ctx, w_mod, b_mod, norm1_g, w_in, ssd_conv_w, ssd_conv_b, ssd_dt_bias,
              ssd_A_log, ssd_D, ssd_norm_g, gdn_conv_w, gdn_dt_bias, gdn_A_log, gdn_norm_g, w_out,
              norm2_g, w_mlp1, w_mlp2, final_g):
    for l in range(DEPTH):
        ctx_out = l < DEPTH - 1
        mod_lat = (jax.nn.silu(c) @ w_mod[l] + b_mod[l])[:, None, :]
        mod_ctx = jax.nn.silu(c_ctx) @ w_mod[l] + b_mod[l]
        sh1, sc1, g1, sh2, sc2, g2 = jnp.split(mod_lat, 6, axis=-1)
        sh1c, sc1c, g1c, sh2c, sc2c, g2c = jnp.split(mod_ctx, 6, axis=-1)
        p_lat = modulate(rmsnorm(x, norm1_g[l]), sh1, sc1) @ w_in[l]
        p_ctx = modulate(rmsnorm(ctx, norm1_g[l]), sh1c, sc1c) @ w_in[l]
        y_lat, y_ctx = token_mixers(p_lat, p_ctx, ssd_conv_w[l], ssd_conv_b[l], ssd_dt_bias[l],
                                    ssd_A_log[l], ssd_D[l], ssd_norm_g[l], gdn_conv_w[l],
                                    gdn_dt_bias[l], gdn_A_log[l], gdn_norm_g[l], ctx_out)
        x = x + g1 * (y_lat @ w_out[l])
        x = x + g2 * sq_relu_mlp(modulate(rmsnorm(x, norm2_g[l]), sh2, sc2), w_mlp1[l], w_mlp2[l])
        if ctx_out:
            ctx = ctx + g1c * (y_ctx @ w_out[l])
            ctx = ctx + g2c * sq_relu_mlp(modulate(rmsnorm(ctx, norm2_g[l]), sh2c, sc2c), w_mlp1[l], w_mlp2[l])
    return rmsnorm(x, final_g)


_first_inputs = first_inputs


def first_inputs(seed=0):
    import zlib

    import numpy as np

    out = dict(_first_inputs(seed))
    spreads = {}
    factors = {'ctx': 6.154,
     'c_ctx': 8.0,
     'b_mod': 3.194,
     'norm1_g': 7.286,
     'ssd_conv_b': 64.0,
     'ssd_D': 64.0,
     'ssd_norm_g': 64.0,
     'gdn_norm_g': 21.57,
     'norm2_g': 17.724,
     'final_g': 8.01}
    for name, (base, spread) in spreads.items():
        noise = np.random.default_rng([zlib.crc32(name.encode()), seed]).standard_normal(out[name].shape)
        drawn = base * np.exp(spread * noise) if base else spread * noise
        out[name] = __import__('jax').numpy.asarray(drawn.astype(out[name].dtype))
    for name, factor in factors.items():
        out[name] = (out[name] * factor).astype(out[name].dtype)
    return out


_narrow_inputs = first_inputs


def first_inputs(seed=0):

    out = dict(_narrow_inputs(seed))
    wider = {'ssd_D': 12.0, 'ssd_norm_g': 5.6, 'gdn_norm_g': 3.3, 'final_g': 3.17}
    for name, times in wider.items():
        mean = out[name].mean()
        out[name] = (mean + times * (out[name] - mean)).astype(out[name].dtype)
    return out


DEPTH_2 = 2

MLA_HEADS = 8
QK_NOPE_DIM = 64
QK_ROPE_DIM = 32
V_HEAD_DIM = 64
Q_LORA_RANK = 384
KV_LORA_RANK = 256
ROPE_THETA = 10000.0
Q_BLOCK = 128
MLA_WIDTH = MLA_HEADS * V_HEAD_DIM
POOL_WINDOWS = (2, 4, 8, 16)
POOL_GROUP_DIM = 64
POOL_WIDTH = len(POOL_WINDOWS) * POOL_GROUP_DIM
SG_HEADS = 4
SG_HEAD_DIM = 64
SG_WIDTH = SG_HEADS * SG_HEAD_DIM
SG_CHUNK = 128
D_MIX = MLA_WIDTH + POOL_WIDTH + SG_WIDTH
IN_COLS = Q_LORA_RANK + KV_LORA_RANK + QK_ROPE_DIM + POOL_WIDTH + 2 * SG_WIDTH
D_FF_2 = -(-(8 * D_MODEL) // (3 * 256)) * 256


def rmsnorm_2(x, g):
    xf = x.astype(jnp.float32)
    y = xf * lax.rsqrt(jnp.mean(xf * xf, axis=-1, keepdims=True) + EPS)
    return (y * g.astype(jnp.float32)).astype(x.dtype)

def rope_tables(positions):
    inv_freq = ROPE_THETA ** (-jnp.arange(0, QK_ROPE_DIM, 2, dtype=jnp.float32) / QK_ROPE_DIM)
    ang = positions.astype(jnp.float32)[..., None] * inv_freq
    return jnp.cos(ang), jnp.sin(ang)

def apply_rope(t, cos, sin):
    tf = t.astype(jnp.float32)
    half = QK_ROPE_DIM // 2
    t1, t2 = tf[..., :half], tf[..., half:]
    out = jnp.concatenate([t1 * cos - t2 * sin, t1 * sin + t2 * cos], axis=-1)
    return out.astype(t.dtype)

def mla_mixer(h_q, h_kv, k_rope_in, positions, q_norm_g, kv_norm_g, w_uq, w_ukv):
    B, S, _ = h_q.shape
    cq = rmsnorm_2(h_q, q_norm_g)
    q = jnp.einsum('bsr,rn->bsn', cq, w_uq).reshape(B, S, MLA_HEADS, QK_NOPE_DIM + QK_ROPE_DIM)
    q_nope, q_rope = q[..., :QK_NOPE_DIM], q[..., QK_NOPE_DIM:]
    ckv = rmsnorm_2(h_kv, kv_norm_g)
    kv = jnp.einsum('bsr,rn->bsn', ckv, w_ukv).reshape(B, S, MLA_HEADS, QK_NOPE_DIM + V_HEAD_DIM)
    k_nope, v = kv[..., :QK_NOPE_DIM], kv[..., QK_NOPE_DIM:]
    cos, sin = rope_tables(positions)
    q_rope = apply_rope(q_rope, cos[:, :, None, :], sin[:, :, None, :])
    k_rope = apply_rope(k_rope_in, cos, sin)
    scale = (QK_NOPE_DIM + QK_ROPE_DIM) ** -0.5
    nb = S // Q_BLOCK

    def blockify(t):
        return jnp.moveaxis(t.reshape(B, nb, Q_BLOCK, *t.shape[2:]), 1, 0)

    def attend(blk):
        qn, qr = blk
        s = (jnp.einsum('bqhd,bkhd->bhqk', qn, k_nope)
             + jnp.einsum('bqhr,bkr->bhqk', qr, k_rope))
        p = jax.nn.softmax(s.astype(jnp.float32) * scale, axis=-1).astype(v.dtype)
        return jnp.einsum('bhqk,bkhd->bqhd', p, v)

    o = lax.map(attend, (blockify(q_nope), blockify(q_rope)))
    return jnp.moveaxis(o, 0, 1).reshape(B, S, MLA_WIDTH)

def pool_mixer(h, w_pool, pool_scale):
    B, S, _ = h.shape
    hf = h.astype(jnp.float32)
    cs = jnp.concatenate([jnp.zeros((B, 1, POOL_WIDTH), jnp.float32), lax.cumsum(hf, axis=1)], axis=1)
    t = jnp.arange(S)
    outs = []
    for g, w in enumerate(POOL_WINDOWS):
        left = w // 2
        right = w - 1 - left
        lo = jnp.clip(t - left, 0, S)
        hi = jnp.clip(t + right + 1, 0, S)
        sl = slice(g * POOL_GROUP_DIM, (g + 1) * POOL_GROUP_DIM)
        csg = cs[:, :, sl]
        mean = (csg[:, hi] - csg[:, lo]) / (hi - lo).astype(jnp.float32)[None, :, None]
        d = (mean - hf[:, :, sl]).astype(h.dtype)
        outs.append(jnp.einsum('bsc,cd->bsd', d, w_pool[g]))
    return jnp.concatenate(outs, axis=-1) * pool_scale

def sg_mixer(h_uv, sg_norm_g, w_s, b_s):
    B, S, _ = h_uv.shape
    z = jax.nn.gelu(h_uv)
    u, v = z[..., :SG_WIDTH], z[..., SG_WIDTH:]
    v = rmsnorm_2(v.reshape(B, S, SG_HEADS, SG_HEAD_DIM), sg_norm_g.reshape(SG_HEADS, SG_HEAD_DIM))
    vc = v.reshape(B, S // SG_CHUNK, SG_CHUNK, SG_HEADS, SG_HEAD_DIM)
    mixed = jnp.einsum('gpq,bcqgd->bcpgd', w_s, vc) + b_s.T[None, None, :, :, None]
    return u * mixed.reshape(B, S, SG_WIDTH)

def second_inputs(seed: int = 0) -> dict:
    key = jax.random.key(seed)
    ks = jax.random.split(key, 20)
    f32 = jnp.float32

    def nrm(k, shape, fan_in):
        return jax.random.normal(k, shape, f32) * (fan_in ** -0.5)

    def gain(k, shape):
        return 1.0 + 0.05 * jax.random.normal(k, shape, f32)

    x = jax.random.normal(ks[0], (BATCH, SEQ, D_MODEL), f32)
    positions = jnp.broadcast_to(jnp.arange(SEQ, dtype=jnp.int32), (BATCH, SEQ))
    return {
        "x": x,
        "positions": positions,
        "mix_norm": gain(ks[1], (DEPTH_2, D_MODEL)),
        "w_in": nrm(ks[2], (DEPTH_2, D_MODEL, IN_COLS), D_MODEL),
        "q_norm": gain(ks[3], (DEPTH_2, Q_LORA_RANK)),
        "kv_norm": gain(ks[4], (DEPTH_2, KV_LORA_RANK)),
        "w_uq": nrm(ks[5], (DEPTH_2, Q_LORA_RANK, MLA_HEADS * (QK_NOPE_DIM + QK_ROPE_DIM)), Q_LORA_RANK),
        "w_ukv": nrm(ks[6], (DEPTH_2, KV_LORA_RANK, MLA_HEADS * (QK_NOPE_DIM + V_HEAD_DIM)), KV_LORA_RANK),
        "w_pool": nrm(ks[7], (DEPTH_2, len(POOL_WINDOWS), POOL_GROUP_DIM, POOL_GROUP_DIM), POOL_GROUP_DIM),
        "pool_scale": gain(ks[8], (DEPTH_2, POOL_WIDTH)),
        "sg_norm": gain(ks[9], (DEPTH_2, SG_WIDTH)),
        "w_s": nrm(ks[10], (DEPTH_2, SG_HEADS, SG_CHUNK, SG_CHUNK), SG_CHUNK),
        "b_s": 1.0 + 0.05 * jax.random.normal(ks[11], (DEPTH_2, SG_HEADS, SG_CHUNK), f32),
        "w_o": nrm(ks[12], (DEPTH_2, D_MIX, D_MODEL), D_MIX),
        "ffn_norm": gain(ks[13], (DEPTH_2, D_MODEL)),
        "w_gate": nrm(ks[14], (DEPTH_2, D_MODEL, D_FF_2), D_MODEL),
        "w_up": nrm(ks[15], (DEPTH_2, D_MODEL, D_FF_2), D_MODEL),
        "w_down": nrm(ks[16], (DEPTH_2, D_FF_2, D_MODEL), D_FF_2),
        "final_norm": gain(ks[17], (D_MODEL,)),
    }

def second_block(x, positions, mix_norm, w_in, q_norm, kv_norm, w_uq, w_ukv, w_pool, pool_scale,
              sg_norm, w_s, b_s, w_o, ffn_norm, w_gate, w_up, w_down, final_norm):
    o1 = Q_LORA_RANK
    o2 = o1 + KV_LORA_RANK
    o3 = o2 + QK_ROPE_DIM
    o4 = o3 + POOL_WIDTH
    for l in range(DEPTH_2):
        h = rmsnorm_2(x, mix_norm[l])
        p = jnp.einsum('bsd,dn->bsn', h, w_in[l])
        a = mla_mixer(p[..., :o1], p[..., o1:o2], p[..., o2:o3], positions,
                      q_norm[l], kv_norm[l], w_uq[l], w_ukv[l])
        b = pool_mixer(p[..., o3:o4], w_pool[l], pool_scale[l])
        c = sg_mixer(p[..., o4:], sg_norm[l], w_s[l], b_s[l])
        mix = jnp.concatenate([a, b, c], axis=-1)
        x = x + jnp.einsum('bsn,nd->bsd', mix, w_o[l])
        h = rmsnorm_2(x, ffn_norm[l])
        g = jnp.einsum('bsd,df->bsf', h, w_gate[l])
        u = jnp.einsum('bsd,df->bsf', h, w_up[l])
        x = x + jnp.einsum('bsf,fd->bsd', jax.nn.silu(g) * u, w_down[l])
    return rmsnorm_2(x, final_norm)


def setup_inputs(seed=0):
    out = dict(first_inputs(seed))
    for name, value in second_inputs(seed + 1).items():
        if name != "x":
            out[name + "_2"] = value
    return out


def reference(
    x, c, ctx, c_ctx, w_mod, b_mod, norm1_g, w_in, ssd_conv_w, ssd_conv_b, ssd_dt_bias,
    ssd_A_log, ssd_D, ssd_norm_g, gdn_conv_w, gdn_dt_bias, gdn_A_log, gdn_norm_g, w_out,
    norm2_g, w_mlp1, w_mlp2, final_g, positions_2, mix_norm_2, w_in_2, q_norm_2, kv_norm_2,
    w_uq_2, w_ukv_2, w_pool_2, pool_scale_2, sg_norm_2, w_s_2, b_s_2, w_o_2, ffn_norm_2,
    w_gate_2, w_up_2, w_down_2, final_norm_2,
):
    x = first_block(
        x, c, ctx, c_ctx, w_mod, b_mod, norm1_g, w_in, ssd_conv_w, ssd_conv_b, ssd_dt_bias,
        ssd_A_log, ssd_D, ssd_norm_g, gdn_conv_w, gdn_dt_bias, gdn_A_log, gdn_norm_g, w_out,
        norm2_g, w_mlp1, w_mlp2, final_g,
    )
    return second_block(
        x, positions_2, mix_norm_2, w_in_2, q_norm_2, kv_norm_2, w_uq_2, w_ukv_2, w_pool_2,
        pool_scale_2, sg_norm_2, w_s_2, b_s_2, w_o_2, ffn_norm_2, w_gate_2, w_up_2, w_down_2,
        final_norm_2,
    )


_drawn_inputs = setup_inputs


def setup_inputs(seed=0):
    import zlib

    import numpy as np

    out = dict(_drawn_inputs(seed))
    spreads = {}
    factors = {'ssd_D': 8.0,
     'mix_norm_2': 8.0,
     'q_norm_2': 8.0,
     'kv_norm_2': 8.0,
     'w_uq_2': 6.133,
     'pool_scale_2': 8.0,
     'sg_norm_2': 8.0,
     'b_s_2': 8.0,
     'ffn_norm_2': 7.516}
    for name, (base, spread) in spreads.items():
        noise = np.random.default_rng([zlib.crc32(name.encode()), seed]).standard_normal(out[name].shape)
        drawn = base * np.exp(spread * noise) if base else spread * noise
        out[name] = __import__('jax').numpy.asarray(drawn.astype(out[name].dtype))
    for name, factor in factors.items():
        out[name] = (out[name] * factor).astype(out[name].dtype)
    return out
```

```python
import numpy as np
from contextlib import ExitStack

import concourse.bass as bass
from concourse import mybir

F32, F32R, BF16, I32 = mybir.dt.float32, mybir.dt.float32r, mybir.dt.bfloat16, mybir.dt.int32
ACT = mybir.ActivationFunctionType
ALU = mybir.AluOpType
AX = mybir.AxisListType

P = 128
D = 1024
KB = D // P
CTX, LAT = 256, 512
TOK = CTX + LAT
CH = 128
NCH = TOK // CH
NCTX = CTX // CH
ROW = 64
SH = 16
GH, GK = 8, 128
NH = SH + GH
TAPS = 5
EPS = 1e-6
FF2 = 2816
QR, KVR, RD = 384, 256, 32
MH, MN = 8, 64
NEG = -1e30
CONVW = 2 + CTX + 2 + (LAT // ROW) * (ROW + 2)
LEVELS = 7


def jobs():
    out = [("qkvx", 8, 34, 1), ("zg", 8, 16, 1), ("wout", 8, 16, 2)]
    for j in range(4):
        out += [(f"up{j}", 8, 8, 1), (f"down{j}", 8, 8, 1)]
    for l in range(2):
        out += [(f"win{l}", 8, 12, 1), (f"uq{l}", 3, 8, 1), (f"uk{l}", 2, 4, 1), (f"uv{l}", 4, 2, 1),
                (f"wo{l}", 8, 8, 1)]
        for j in range(3):
            n = 8 if j < 2 else FF2 // P - 16
            out += [(f"gu{l}{j}", 8, 2 * n, 1), (f"dn{l}{j}", n, 8, 1)]
    return out


JOBS = jobs()


class Job:
    def __init__(self, i):
        self.name, self.kc, self.n, self.per = JOBS[i]
        self.u0 = sum(j[2] for j in JOBS[:i])
        self.b0 = sum(j[2] // j[3] for j in JOBS[:i] if not j[0].startswith("uv"))
        self.next_kc = JOBS[i + 1][1] if i + 1 < len(JOBS) else None


JOB = {j[0]: Job(i) for i, j in enumerate(JOBS)}


CF = ["ident", "incl_f", "incl_b", "rest_f", "rest_b", "ones", "half"]
NB = 3 + 2 * LEVELS


def constants():
    i = np.arange(P)
    k, j = i[:, None], i[None, :]
    f = {"ident": k == j, "incl_f": k <= j, "incl_b": k >= j, "rest_f": k > j, "rest_b": k < j,
         "ones": k + j >= 0, "half": k // 64 == j // 64}
    cf = np.concatenate([f[n].astype(np.float32) for n in CF], axis=1)
    neg = [np.where(j >= k, 0.0, NEG), np.where(j <= k, 0.0, NEG)]
    lv = []
    for d in range(2):
        for s in range(LEVELS):
            b = 1 << s
            src, dst = (k, j) if d == 0 else (j, k)
            lv.append(((src // (2 * b) == dst // (2 * b)) & (src // b % 2 == 0) & (dst // b % 2 == 1)).astype(np.float32))
    cb = np.concatenate([(k == j).astype(np.float32)] + neg + lv, axis=1)
    inv = 10000.0 ** (-np.arange(0, RD, 2, dtype=np.float32) / RD)
    fr = np.zeros((P, 3), np.float32)
    fr[:64, 0] = np.tile(inv, 4)
    fr[:32, 1] = np.pi / 2
    fr[:, 2] = 1.0
    fr[32:48, 2] = -1.0
    t = np.arange(LAT)
    cnt = np.zeros((P, 2, LAT), np.float32)
    for g, w in enumerate((2, 4, 8, 16)):
        n = np.clip(t + w - w // 2, 0, LAT) - np.clip(t - w // 2, 0, LAT)
        cnt[64 * (g % 2):64 * (g % 2) + 64, g // 2] = 1.0 / n
    return cf, cb, fr, cnt


VEC = [("c", 16), ("b_mod", 48), ("norm1", 8), ("norm2", 8), ("final1", 8), ("ssdn", 8), ("gdnn", 1),
       ("convw", 34 * TAPS), ("convb", 34), ("mixn0", 8), ("mixn1", 8), ("qn0", 3), ("qn1", 3),
       ("kvn0", 2), ("kvn1", 2), ("psc0", 2), ("psc1", 2), ("sgn0", 2), ("sgn1", 2), ("ffn0", 8), ("ffn1", 8),
       ("final2", 8), ("freq", 3), ("bias", 48), ("alog", 48), ("ssdD", 16)]
VOFF, _o = {}, 0
for _n, _k in VEC:
    VOFF[_n] = (_o, _k)
    _o += _k
NVEC = _o


def layout(x, c, ctx, c_ctx, w_mod, b_mod, norm1_g, w_in, ssd_conv_w, ssd_conv_b, ssd_dt_bias, ssd_A_log,
           ssd_D, ssd_norm_g, gdn_conv_w, gdn_dt_bias, gdn_A_log, gdn_norm_g, w_out, norm2_g, w_mlp1,
           w_mlp2, final_g, positions_2, mix_norm_2, w_in_2, q_norm_2, kv_norm_2, w_uq_2, w_ukv_2,
           w_pool_2, pool_scale_2, sg_norm_2, w_s_2, b_s_2, w_o_2, ffn_norm_2, w_gate_2, w_up_2, w_down_2,
           final_norm_2):
    def units(w, cols=None, k0=0, kc=None):
        w = np.asarray(w)
        w = w if cols is None else w[:, cols]
        kc = kc or w.shape[0] // P
        w = w[k0 * P:(k0 + kc) * P]
        return np.ascontiguousarray(w.reshape(kc, P, -1, P).transpose(2, 1, 0, 3).reshape(-1, P, kc * P))

    def col(v):
        return np.asarray(v).reshape(-1, P).T

    a = {}
    w_in = np.asarray(w_in)[0]
    oz, ox, odt, oq, og, oa, ob = np.cumsum([0, 1024, 1280, 32, 3072, 1024, 16]).tolist()
    r = np.arange
    cols = np.concatenate([oq + 1024 + r(2048), ox + r(1280), oq + r(1024)])
    stream = {"qkvx": units(w_in, cols), "zg": units(w_in, np.concatenate([oz + r(1024), og + r(1024)]))}
    small = np.concatenate([odt + r(16), oa + r(8), odt + 16 + r(16), oa + 8 + r(8), ob + r(16)])
    a["w_small"] = np.ascontiguousarray(w_in[:, small].reshape(KB, P, 64).transpose(1, 0, 2).reshape(P, KB * 64))
    a["w_mod"] = units(np.asarray(w_mod)[0])
    wo = np.asarray(w_out)[0]
    halves = [units(wo, k0=8 * i, kc=8) for i in range(2)]
    stream["wout"] = np.stack(halves, 1).reshape(16, P, 1024)
    for j in range(4):
        stream[f"up{j}"] = units(np.asarray(w_mlp1)[0], 1024 * j + r(1024))
        stream[f"down{j}"] = units(np.asarray(w_mlp2)[0], k0=8 * j, kc=8)
    for l in range(2):
        w2 = np.asarray(w_in_2)[l]
        t1, t2 = 640 + r(16), 656 + r(16)
        cols = np.concatenate([r(640), t1, t2, t2, t1, 672 + r(64), 672 + r(768)])
        stream[f"win{l}"] = units(w2, cols)
        cols = np.concatenate([np.concatenate([96 * h + 64 + r(16), 96 * h + 80 + r(16), 96 * h + 80 + r(16),
                                               96 * h + 64 + r(16), 96 * h + r(64)]) for h in range(MH)])
        stream[f"uq{l}"] = units(np.asarray(w_uq_2)[l], cols)
        wk = np.asarray(w_ukv_2)[l]
        stream[f"uk{l}"] = units(wk, np.concatenate([128 * h + r(64) for h in range(MH)]))
        stream[f"uv{l}"] = np.ascontiguousarray(
            wk[:, np.concatenate([128 * h + 64 + r(64) for h in range(MH)])].reshape(2, P, 512))
        stream[f"wo{l}"] = units(np.asarray(w_o_2)[l])
        g, u = units(np.asarray(w_gate_2)[l]), units(np.asarray(w_up_2)[l])
        gu = np.stack([g, u], 1).reshape(-1, P, 1024)
        for j in range(3):
            n = 8 if j < 2 else FF2 // P - 16
            stream[f"gu{l}{j}"] = gu[16 * j:16 * j + 2 * n]
            stream[f"dn{l}{j}"] = units(np.asarray(w_down_2)[l], k0=8 * j, kc=n)
    for name, kc, n, per in JOBS:
        a["s_" + name] = np.ascontiguousarray(stream[name])
        assert a["s_" + name].shape == (n, P, kc * P), name

    xt = np.concatenate([np.asarray(ctx)[0], np.asarray(x)[0]], 0).T
    a["xt"] = np.ascontiguousarray(xt.reshape(KB, P, TOK).transpose(1, 0, 2).reshape(P, KB * TOK))
    a["cf"], a["cb"], fr, cnt = constants()
    a["cb"] = a["cb"].astype(mybir.dt.np(BF16))
    a["cnt"] = cnt.reshape(P, 2 * LAT)
    cw = np.concatenate([np.asarray(gdn_conv_w)[0][:, 1024:], np.asarray(ssd_conv_w)[0],
                         np.asarray(gdn_conv_w)[0][:, :1024]], 1)
    cbias = np.concatenate([np.zeros(2048, np.float32), np.asarray(ssd_conv_b)[0], np.zeros(1024, np.float32)])
    rep = lambda v: np.broadcast_to(np.asarray(v).reshape(1, -1), (P, np.asarray(v).size))
    dtb, gb = np.asarray(ssd_dt_bias)[0], np.asarray(gdn_dt_bias)[0]
    sa, ga = np.asarray(ssd_A_log)[0], np.asarray(gdn_A_log)[0]
    v = {"c": np.stack([col(np.asarray(c)[0]), col(c_ctx)], 2).reshape(P, 16), "b_mod": col(np.asarray(b_mod)[0]),
         "norm1": col(np.asarray(norm1_g)[0]), "norm2": col(np.asarray(norm2_g)[0]), "final1": col(final_g),
         "ssdn": col(np.asarray(ssd_norm_g)[0]), "gdnn": col(np.asarray(gdn_norm_g)[0]),
         "convw": cw.reshape(TAPS, 34, P).transpose(2, 1, 0).reshape(P, 34 * TAPS), "convb": col(cbias),
         "final2": col(final_norm_2), "freq": fr,
         "bias": rep(np.concatenate([dtb[0], gb[0], dtb[1], gb[1]])),
         "alog": rep(np.concatenate([sa[0], ga[0], sa[1], ga[1]])), "ssdD": rep(np.asarray(ssd_D)[0])}
    for l in range(2):
        v[f"mixn{l}"], v[f"qn{l}"], v[f"kvn{l}"] = (col(np.asarray(t)[l]) for t in (mix_norm_2, q_norm_2, kv_norm_2))
        v[f"psc{l}"], v[f"sgn{l}"], v[f"ffn{l}"] = (col(np.asarray(t)[l]) for t in (pool_scale_2, sg_norm_2, ffn_norm_2))
    a["vec"] = np.ascontiguousarray(np.concatenate([v[n].reshape(P, k) for n, k in VEC], 1))
    a["pos"] = np.ascontiguousarray(np.broadcast_to(np.asarray(positions_2), (64, LAT)))
    a["wpool"] = np.ascontiguousarray(np.asarray(w_pool_2).reshape(2, 2, 2 * 64, 64).transpose(0, 2, 1, 3).reshape(2, P, 128))
    a["ws"] = np.ascontiguousarray(np.asarray(w_s_2).transpose(0, 3, 1, 2).reshape(2, P, 512))
    bs = np.asarray(b_s_2).reshape(2, 2, 2, 1, P)
    a["bs"] = np.ascontiguousarray(np.broadcast_to(bs, (2, 2, 2, 64, P)).transpose(0, 2, 3, 1, 4).reshape(2, P, 256))
    return a


class Need:

    def __init__(self, eng):
        self.eng, self.seen, self.per, self.i, self.off = eng, {}, None, None, {}

    def __call__(self, sem, k=1, lag=0):
        name = sem.name
        if self.per is not None and name in self.per:
            self.off[name] = self.off.get(name, 0) + k
            base = self.seen.get(name, 0) + self.off[name] - lag
            self.eng.wait_ge(sem, self.i * self.per[name] + base)
            return
        self.seen[name] = self.seen.get(name, 0) + k
        if self.seen[name] - lag > 0:
            self.eng.wait_ge(sem, self.seen[name] - lag)

    def skip(self, sem, k=1):
        d = self.off if self.per is not None and sem.name in self.per else self.seen
        d[sem.name] = d.get(sem.name, 0) + k

    def enter(self, i, per):
        self.i, self.per, self.off = i, {s.name: k for s, k in per.items()}, {}

    def leave(self, turns):
        for n, k in self.per.items():
            assert self.off.get(n, 0) == k, (n, self.off.get(n, 0), k)
            self.seen[n] = self.seen.get(n, 0) + k * turns
        self.per = None


def build_kernel(nc, a, out):
    ctx = ExitStack()
    with ctx:
        base = 16512
        tensors = {}

        def at(name, kb, shape, dt=F32):
            tensors[name] = nc.alloc_sbuf_tensor_at(name, [shape[0], int(np.prod(shape[1:]))], dt, offset=base + int(kb * 1024))
            return tensors[name]

        def v3(t, n):
            return t[:, :].rearrange("p (n t) -> p n t", n=n)

        def sem(name):
            return ctx.enter_context(nc.semaphore(name))

        bank = [ctx.enter_context(nc.psum_tensor(f"bank{i}", [P, 512], F32)) for i in range(8)]

        raw = [at(f"raw{s}", 4 * s, (P, 1024)) for s in range(2)]
        whi = [at(f"whi{s}", 8 + 4 * s, (P, 1024), F32R) for s in range(2)]
        wlo = [at(f"wlo{s}", 16 + 4 * s, (P, 1024), F32R) for s in range(2)]
        cf = at("cf", 24, (P, len(CF) * P))
        cb = at("cb", 27.5, (P, NB * P), BF16)
        vec = at("vec", 31.75, (P, NVEC))
        identr = at("identr", 34, (P, P), F32R)
        modv = at("modv", 34.5, (P, 96))
        aff = at("aff", 35, (P, 48))
        assert 31.75 * 1024 + NVEC * 4 <= 34 * 1024

        def const(n):
            i = CF.index(n)
            return cf[:, i * P:(i + 1) * P]

        def cbf(i, n=1):
            return cb[:, i * P:(i + n) * P]

        def vc(n, i=0, k=None):
            o, w = VOFF[n]
            return vec[:, o + i:o + i + (k or w - i)]

        hhi = at("hhi", 36, (P, KB * TOK), F32R)
        hlo = at("hlo", 60, (P, KB * TOK), F32R)
        cbuf = [at(f"cbuf{s}", 84 + 3.125 * s, (P, CONVW)) for s in range(2)]
        cacc = [at(f"cacc{s}", 90.25 + 3.125 * s, (P, CONVW)) for s in range(2)]
        sil = at("sil", 96.5, (P, TOK))
        kf = at("kf", 100, (P, GH * TOK))
        qf = at("qf", 124, (P, GH * LAT))
        vt = at("vt", 140, (P, NCH * GH * GK))
        xtm = at("xtm", 164, (P, NCH * D))
        bf = at("bf", 188, (P, TOK))
        btm = at("btm", 191, (P, NCH * P))
        cfm = at("cfm", 194, (P, LAT))
        st = 196
        stats = {}
        for n, w, dt in (("sp", 288, F32), ("ga", 288, F32), ("beta", 96, F32), ("ng", 288, F32),
                         ("eg", 288, F32), ("er", 288, F32), ("et", 288, F32), ("ghi", 288, F32R),
                         ("glo", 288, F32R), ("eghi", 288, F32R), ("eglo", 288, F32R)):
            stats[n] = at(n, st, (P, w), dt)
            st += w * 4 / 1024
        assert base + st * 1024 <= 229344, st
        lndt = at("lndt", 98, (P, 288))
        g = at("g", 96.5, (P, 288))
        sp, ga, beta, ng, eg, er, et, ghi, glo, eghi, eglo = stats.values()
        xw, neg_eg = ga, sp

        sq2 = [at(f"sq2{s}", 84 + 3 * s, (P, TOK)) for s in range(2)]
        NLEN = GH * NCH + GH * (NCH - NCTX)
        len_root, len_rs = at("len_root", 90.25, (P, NLEN)), at("len_rs", 91, (P, NLEN))
        len_hi, len_lo = at("len_hi", 91.75, (P, NLEN), F32R), at("len_lo", 92.5, (P, NLEN), F32R)

        xt = at("xt", 100, (P, KB * TOK))
        sq = [at(f"sq{s}", 124 + 3 * s, (P, TOK)) for s in range(2)]
        rstd = at("rstd", 130, (P, TOK))
        root = at("root", 133, (P, TOK))
        tmp = [at(f"tmp{s}", 136 + 3 * s, (P, TOK)) for s in range(2)]
        modw = [at(f"modw{s}", 142 + 4 * s, (P, 1024)) for s in range(4)]
        late_modw = [at(f"late_modw{s}", 124 + 4 * s, (P, 1024)) for s in range(4)]
        wsm = at("wsm", 158, (P, 512))
        wsmhi = at("wsmhi", 160, (P, 512), F32R)
        wsmlo = at("wsmlo", 162, (P, 512), F32R)
        cs = at("cs", 34.875, (P, 16))
        xb, ab, ee = (at(n, 165 + 2 * i, (P, 288)) for i, n in enumerate(("xb", "ab", "ee")))
        ea = at("ea", 171, (P, 48))

        raw_loaded = [sem(f"raw_loaded{s}") for s in range(2)]
        hi_ready, lo_ready, unit_done, out_taken = (sem(n) for n in ("hi_ready", "lo_ready", "unit_done", "out_taken"))
        const_loaded, x_loaded, small_loaded = (sem(n) for n in ("const_loaded", "x_loaded", "small_loaded"))
        mod_loaded = [sem(f"mod_loaded{s}") for s in range(4)]
        mod_done, cs_ready = sem("mod_done"), sem("cs_ready")
        identr_ready, pads_ready = sem("identr_ready"), sem("pads_ready")
        sq_ready, sq_used, sum_full, root_ready, scaled, hi_out, lo_out = (
            sem(n) for n in ("sq_ready", "sq_used", "sum_full", "root_ready", "scaled", "hi_out", "lo_out"))
        smallw_hi, smallw_ready, small_full, small_act, cum_full = (
            sem(n) for n in ("smallw_hi", "smallw_ready", "small_full", "small_act", "cum_full"))
        cb_ready, conv_done, sil_ready, tm_full, tm_taken = (
            sem(n) for n in ("cb_ready", "conv_done", "sil_ready", "tm_full", "tm_taken"))
        pool_done = sem("pool_done")
        dve_done, act_done, phase_end = sem("dve_done"), sem("act_done"), sem("phase_end")
        zg_stored = [sem(f"zg_stored{s}") for s in range(2)]

        small_dve, small_ln = sem("small_dve"), sem("small_ln")
        len_rooted, len_inverse, len_hi_ready, len_lo_ready, bc_full, bc_used = (
            sem(n) for n in ("len_rooted", "len_inverse", "len_hi_ready", "len_lo_ready", "bc_full", "bc_used"))
        zg_dram = nc.dram_tensor("zg_scratch", (16, P, LAT), F32).ap()


        def barrier(eng, n):
            eng.drain().then_inc(phase_end, 1)
            eng.wait_ge(phase_end, 4 * n)

        def has_ctx(u):
            return u < 25

        def conv_ops(u):
            return sum(2 if has_ctx(w) else 1 for w in range(u))

        def late_mods(u):
            return range(16 + (u - 2) * 4 // 3, 16 + (u - 1) * 4 // 3) if 2 <= u < 26 else ()

        def len_col(h, c):
            return h * NCH + c if h < GH else GH * NCH + (h - GH) * (NCH - NCTX) + c - NCTX

        def rows(t, off=0):
            return t[:, off:off + 8 * 66].rearrange("p (r c) -> p r c", r=8)[:, :, 0:ROW]

        def in_turns(eng, need, job, per, body, peel=False):
            n = job.n // job.per
            first = int(peel or job.name == "zg")
            turns = n // 2 - 1 - first
            for b in range(2 * first):
                body(b, b % 2, False)
            if turns > 1:
                with eng.Fori(first, first + turns) as i:
                    need.enter(i - first if first else i, per)
                    for k in range(2):
                        body(i * 2 + k, k, False)
                    need.leave(turns)
            else:
                turns = 0
            for b in range(2 * (first + turns), n):
                body(b, b % 2, b == n - 1)

        def pe_products(pe, need, u, k, out, rhi, rlo, kc, cols, start=True, stop=True, each=None):
            pe.wait_ge(hi_ready, u + 1)
            pe.wait_ge(lo_ready, u + 1)
            for s in range(kc):
                if each is not None:
                    need(each)
                w_hi, w_lo = whi[k][:, s * P:(s + 1) * P], wlo[k][:, s * P:(s + 1) * P]
                pe.matmul(out, w_hi, rhi(s), start=start and s == 0, stop=False)
                pe.matmul(out, w_hi, rlo(s), start=False, stop=False)
                mm = pe.matmul(out, w_lo, rhi(s), start=False, stop=stop and s == kc - 1)
            mm.then_inc(unit_done, 1)

        def split_hi(act, u, k, kc):
            act.wait_ge(raw_loaded[k], 16 * (u // 2 + 1) if isinstance(u, int) else u * 8 + (16 - 8 * k))
            if not isinstance(u, int) or u >= 2:
                act.wait_ge(unit_done, u - 1)
            act.activation(whi[k][:, 0:kc * P], raw[k][:, 0:kc * P], ACT.Identity).then_inc(hi_ready, 1)

        def split_lo(dve, u, k, kc):
            dve.wait_ge(hi_ready, u + 1)
            if not isinstance(u, int) or u >= 2:
                dve.wait_ge(unit_done, u - 1)
            dve.tensor_tensor(wlo[k][:, 0:kc * P], raw[k][:, 0:kc * P], whi[k][:, 0:kc * P].bitcast(F32),
                              ALU.subtract).then_inc(lo_ready, 1)

        def split_next(split, eng, job, b, k, last):
            if not last:
                split(eng, b + (job.u0 + 1), 1 - k, job.kc)
            elif job.next_kc:
                split(eng, job.u0 + job.n, 0, job.next_kc)

        stg = [at(f"stg{s}", 84 + 2 * s, (P, LAT)) for s in range(2)]
        hst = at("hst", 36, (P, 8 * 512))
        xwb = [at(f"xwb{s}", 52 + 4 * s, (P, D)) for s in range(2)]
        ebc = [at(f"ebc{s}", 52 + 4 * s, (P, D), F32R) for s in range(2)]
        wmat = at("wmat", 60, (P, SH * P))
        lbuf = [at(f"lbuf{s}", 68 + 2 * s, (P, 512)) for s in range(2)]
        stb = at("stb", 72, (P, 256))
        cpm = at("cpm", 73, (P, 16 * P))
        yfm = at("yfm", 81, (P, KB * LAT))
        etb = at("etb", 97, (P, 96))
        htmp = at("htmp", 98, (P, 512))
        S, DEC, AT, Dm, DT = ([at(f"{n}{q}", 36 + 8 * i + 2 * q, (P, 512)) for q in range(4)]
                              for i, n in enumerate(("S", "DEC", "AT", "Dm", "DT")))
        PM, CS, KD, VN = ([at(f"{n}{q}", 164 + 8 * i + 2 * q, (P, 512)) for q in range(4)]
                          for i, n in enumerate(("PM", "CS", "KD", "VN")))
        RM, QE, QKD = CS, Dm, AT
        ofm = at("ofm", 81, (P, GH * LAT))
        neg_eg = at("neg_eg", 97, (P, 288))

        scan_names = ("xw_ready", "st_full", "st_taken", "sc_full", "sc_copied", "cp_full", "cp_ready", "l_full", "l_ready",
                   "w_ready", "y_full", "y_taken", "y_spilled", "ktm_full", "kd_ready", "gb_full", "dec_ready", "gram_full",
                   "at_ready", "c_ready", "c1_full", "dt_ready", "d_ready", "p_full", "p_ready", "dp_full", "dtp_full",
                   "egb_full", "qe_ready", "qk_full", "qkd_ready", "ks_full", "r_ready", "dr_full", "vn_ready", "o_full",
                   "o_added", "s_full", "s_ready", "eb_ready")
        (xw_ready, st_full, st_taken, sc_full, sc_copied, cp_full, cp_ready, l_full, l_ready, w_ready, y_full, y_taken,
         y_spilled, ktm_full, kd_ready, gb_full, dec_ready, gram_full, at_ready, c_ready, c1_full, dt_ready, d_ready,
         p_full, p_ready, dp_full, dtp_full, egb_full, qe_ready, qk_full, qkd_ready, ks_full, r_ready, dr_full, vn_ready,
         o_full, o_added, s_full, s_ready, eb_ready) = (sem(n) for n in scan_names)
        y_dram = nc.dram_tensor("y_scratch", (P, KB * LAT), F32).ap()

        SSEQ = ((0, 1, 2, 3, 4), (1, 0, 5, 4, 3))
        GSEQ = ((0, 1, 2, 3, 4, 5), (1, 0, 5, 4, 3, 2))

        def dcol(d, c, h=0):
            return (d * NCH + c) * NH + h

        def ex(ap, n):
            return ap.broadcast_to((P, n))

        def b4(ap, n=4):
            return ap.unsqueeze(1).broadcast_to((P, n, ap.shape[1]))

        def h4(t, n=4):
            return t.rearrange("p (h t) -> p h t", h=n)

        def scal4(ap, w):
            return ap.unsqueeze(2).broadcast_to((P, ap.shape[1], w))

        zb, gateb = at("zb", 36, (P, KB * LAT)), at("gateb", 52, (P, KB * LAT))
        yb = at("yb", 100, (P, KB * LAT))
        yhi, ylo = at("yhi", 116, (P, 16 * LAT), F32R), at("ylo", 148, (P, 16 * LAT), F32R)
        xr = at("xr", 180, (P, KB * LAT))
        xhi, xlo = at("xhi", 36, (P, KB * LAT), F32R), at("xlo", 52, (P, KB * LAT), F32R)
        fhi, flo = at("fhi", 68, (P, KB * LAT), F32R), at("flo", 84, (P, KB * LAT), F32R)
        work = {}
        for nm, kb in (("a", 68), ("b", 100)):
            work[nm] = [[at(f"{n}{nm}{s}", kb + 4 * i + 2 * s, (P, LAT)) for s in range(2)]
                        for i, n in enumerate(("sqm", "rsm", "tpm"))]
        MN_ = (2 + GH) * 4
        mn_root, mn_rs = at("mn_root", 99, (P, MN_)), at("mn_rs", 99.25, (P, MN_))
        mn_hi, mn_lo = at("mn_hi", 99.5, (P, MN_), F32R), at("mn_lo", 99.75, (P, MN_), F32R)
        lnb = at("lnb", 203.75, (P, LAT))
        rt = [at(f"rt{s}", 112 + 2 * s, (P, LAT)) for s in range(2)]
        pf = at("pf", 116, (P, 12 * LAT))
        chi, clo = at("chi", 140, (P, 5 * LAT), F32R), at("clo", 150, (P, 5 * LAT), F32R)
        qh, kh = at("qh", 68, (P, MH * LAT)), at("kh", 84, (P, MH * LAT))
        vh = at("vh", 160, (P, 4 * LAT))
        eb = [at(f"eb{s}", kb, (P, LAT)) for s, kb in enumerate((156, 168, 170))]
        pt = [at(f"pt{s}", 172 + 2 * s, (P, LAT)) for s in range(2)]
        rope = at("rope", 196, (P, LAT))
        cntb = at("cntb", 198, (P, 2 * LAT))
        bsb = at("bsb", 202, (P, 2 * P))
        wpb = at("wpb", 203, (P, P))
        smal = at("smal", 203.5, (P, 9))
        wsb = at("wsb", 176, (P, 4 * P))
        px = [at(f"px{s}", 140 + 2.25 * s, (P, 528)) for s in range(5)]
        vts = at("vts", 152, (P, 8 * P))
        posb = at("posb", 205.75, (64, LAT), I32)
        ra, rb = (at(n, k, (64, LAT)) for n, k in (("ra", 72), ("rb", 97)))

        block_names = ("q_ready", "q_used", "ln_done", "rs_ready", "t_ready", "t_hi", "t_lo", "back_loaded", "xr_loaded",
                  "v_ready", "relu_ready", "tab_loaded", "rope_step", "rope_sin", "rope_ready", "act_part",
                  "s2_full", "mx_ready", "e_ready", "pn_ready", "tp_full", "pt_ready", "pv_done", "ao_hi", "ao_taken",
                  "pd_ready", "pw_full", "pw_hi", "gelu_ready", "vn2_ready", "vt2_full", "vt2_ready", "sg_full",
                  "out_stored", "uv_taken", "zero_ready", "rs_used")
        (q_ready, q_used, ln_done, rs_ready, t_ready, t_hi, t_lo, back_loaded, xr_loaded, v_ready, relu_ready, tab_loaded,
         rope_step, rope_sin, rope_ready, act_part, s2_full, mx_ready, e_ready, pn_ready, tp_full, pt_ready,
         pv_done, ao_hi, ao_taken, pd_ready, pw_full, pw_hi, gelu_ready, vn2_ready, vt2_full, vt2_ready, sg_full,
         out_stored, uv_taken, zero_ready, rs_used) = (sem(n) for n in block_names)

        def blk(t, b, n=1):
            return t[:, b * LAT:(b + n) * LAT] if isinstance(b, int) else t[:, bass.ds(b * LAT, n * LAT)]

        def pcol(t, b):
            return t[:, b:b + 1] if isinstance(b, int) else t[:, bass.ds(b, 1)]

        QS = 1.0 / float(np.sqrt(np.float32(MN + RD)))

        def mlp_jobs():
            return [(JOB[f"up{j}"], JOB[f"down{j}"]) for j in range(4)]

        def ffn_jobs(l):
            return [(JOB[f"gu{l}{j}"], JOB[f"dn{l}{j}"]) for j in range(3)]
        tiles = nc.Block()
        block = ctx.enter_context(tiles)

        @block.sync
        def _(sp_):
            for t, s in ((vec, "vec"), (cf, "cf"), (cb, "cb")):
                sp_.dma_start(t[:, :], a[s]).then_inc(const_loaded, 16)
            sp_.dma_start(xt[:, :], a["xt"]).then_inc(x_loaded, 16)
            for u in range(4):
                sp_.dma_start(modw[u][:, :], a["w_mod"][u]).then_inc(mod_loaded[u], 16)
            sp_.dma_start(wsm[:, :], a["w_small"]).then_inc(small_loaded, 16)
            with sp_.Fori(0, 3) as i:
                for s in range(4):
                    sp_.wait_ge(mod_done, i * 4 + (s + 1))
                    sp_.dma_start(modw[s][:, :], a["w_mod"][bass.ds(i * 4 + (s + 4), 1)].rearrange("o p n -> (o p) n")
                                  ).then_inc(mod_loaded[s], 16)

            def stream(job):
                def load(j, k):
                    u = j + job.u0
                    if not isinstance(u, int) or u >= 2:
                        sp_.wait_ge(hi_ready, u - 1)
                        sp_.wait_ge(lo_ready, u - 1)
                    src = a["s_" + job.name]
                    src = src[j] if isinstance(j, int) else src[bass.ds(j, 1)].rearrange("o p n -> (o p) n")
                    sp_.dma_start(raw[k][:, 0:job.kc * P], src).then_inc(raw_loaded[k], 16)

                first = 0
                if job.u0 == 0:
                    for j in range(job.n):
                        load(j, j % 2)
                        for m in late_mods(j):
                            if m == 16:
                                sp_.wait_ge(lo_out, 2 * KB)
                            else:
                                sp_.wait_ge(mod_done, m - 3)
                            sp_.dma_start(late_modw[m % 4][:, :], a["w_mod"][m]).then_inc(mod_loaded[m % 4], 16)
                    return
                if (job.n - first) // 2 > 1:
                    with sp_.Fori(0, (job.n - first) // 2) as i:
                        for k in range(2):
                            load(i * 2 + (first + k), k)
                else:
                    for j in range(first, job.n):
                        load(j, j % 2)

            stream(JOB["qkvx"])
            stream(JOB["zg"])
            for j in JOBS[2:]:
                stream(JOB[j[0]])

        @block.tensor
        def _(pe):
            need = Need(pe)
            need(const_loaded, 48)
            need(identr_ready)
            need(cs_ready)

            def pe_sums(need, n, parts, w="ones"):
                for b in range(n):
                    need(sq_ready)
                    for q, (bk, lo, hi) in enumerate(parts):
                        mm = pe.matmul(bk[:, 0:hi - lo], const(w), sq[b % 2][:, lo:hi], start=(b == 0), stop=(b == n - 1))
                    mm.then_inc(sq_used, 1)

            pe_sums(need, KB, [(bank[5], 0, CTX), (bank[4], CTX, TOK)])

            with pe.Fori(0, 4) as i:
                need.enter(i, {m: 16 for m in mod_loaded})
                for s in range(4):
                    need(mod_loaded[s], 16)
                    for k in range(KB):
                        mm = pe.matmul(bank[7][:, bass.ds(i * 8 + 2 * s, 2)], modw[s][:, k * P:(k + 1) * P],
                                       cs[:, 2 * k:2 * k + 2], start=(k == 0), stop=(k == KB - 1))
                    mm.then_inc(mod_done, 1)
                need.leave(4)

            need(root_ready, 2)

            need(smallw_ready)
            need(lo_out, 2 * KB)
            for tt in range(NCH):
                dst = bank[6][:, tt * 64:(tt + 1) * 64]
                for k in range(KB):
                    xh = hhi[:, k * TOK + tt * P:k * TOK + (tt + 1) * P]
                    xl = hlo[:, k * TOK + tt * P:k * TOK + (tt + 1) * P]
                    wh, wl = wsmhi[:, k * 64:(k + 1) * 64], wsmlo[:, k * 64:(k + 1) * 64]
                    pe.matmul(dst, xh, wh, start=(k == 0), stop=False)
                    pe.matmul(dst, xh, wl, start=False, stop=False)
                    mm = pe.matmul(dst, xl, wh, start=False, stop=(k == KB - 1))
            mm.then_inc(small_full, 1)

            job = JOB["qkvx"]
            hh, hl = v3(hhi, KB), v3(hlo, KB)

            def transposes(u):
                pe.wait_ge(sil_ready, conv_ops(u + 1))
                need(tm_taken, 2, lag=2)
                src = bf if u == 24 else sil
                for c in range(NCH):
                    mm = pe.transpose(bank[4 + c // 4][:, (c % 4) * P:(c % 4 + 1) * P], src[:, c * P:(c + 1) * P], const("ident"))
                mm.then_inc(tm_full, 1)

            for u in range(job.n):
                if u >= 2:
                    pe.wait_ge(cb_ready, conv_ops(u - 1))
                k = u % 2
                pe.wait_ge(hi_ready, u + 1)
                pe.wait_ge(lo_ready, u + 1)
                lat, cx = bank[k][:, :], bank[2 + k][:, 0:CTX]
                for s in range(KB):
                    w_hi, w_lo = whi[k][:, s * P:(s + 1) * P], wlo[k][:, s * P:(s + 1) * P]
                    for n, (w, x) in enumerate(((w_hi, hh), (w_hi, hl), (w_lo, hh))):
                        first, last = s == 0 and n == 0, s == KB - 1 and n == 2
                        if has_ctx(u):
                            pe.matmul(cx, w, x[:, s, 0:CTX], start=first, stop=last)
                        mm = pe.matmul(lat, w, x[:, s, CTX:TOK], start=first, stop=last)
                mm.then_inc(unit_done, 1)
                for m in late_mods(u):
                    need(mod_loaded[m % 4], 16)
                    for s in range(KB):
                        mm = pe.matmul(bank[7][:, 2 * m:2 * m + 2], late_modw[m % 4][:, s * P:(s + 1) * P], cs[:, 2 * s:2 * s + 2],
                                       start=(s == 0), stop=(s == KB - 1))
                    mm.then_inc(mod_done, 1)
                if 8 <= u - 2 < 25:
                    transposes(u - 2)

            need(small_act, 1)
            gav = ga[:, :].rearrange("p (c x) -> p c x", c=NCH)
            for d in range(2):
                src = gav[:, :, d * NH:(d + 1) * NH]
                pe.matmul(bank[6][:, d * 144:(d + 1) * 144], const(("incl_f", "incl_b")[d]), src, start=True, stop=True)
            pe.wait_ge(cb_ready, conv_ops(job.n))
            for d in range(2):
                src = gav[:, :, d * NH:(d + 1) * NH]
                pe.matmul(bank[0][:, d * 144:(d + 1) * 144], const(("rest_f", "rest_b")[d]), src, start=True, stop=True)
                mm = pe.matmul(bank[1][:, d * 144:(d + 1) * 144], const("ones"), src, start=True, stop=True)
            mm.then_inc(cum_full, 1)
            for h in range(2 * GH):
                need(sq_ready)
                for c in range(0 if h < GH else NCTX, NCH):
                    o = len_col(h, c)
                    mm = pe.matmul(bank[2][:, o:o + 1], sq2[h % 2][:, c * P:(c + 1) * P], const("ones")[:, 0:1], start=True, stop=True)
                mm.then_inc(sum_full, 1)
            need(len_hi_ready)
            need(len_lo_ready)
            for h in range(2 * GH):
                need(bc_used, 1, lag=2)
                for c in range(0 if h < GH else NCTX, NCH):
                    o = len_col(h, c)
                    dst = bank[4 + h % 2][:, (c - NCTX) * P:(c - NCTX + 1) * P] if c >= NCTX else bank[h % 2][:, c * P:(c + 1) * P]
                    for n, r in enumerate((len_hi, len_lo)):
                        mm = pe.matmul(dst, r[:, o:o + 1].broadcast_to((P, P)), identr[:, :], start=(n == 0), stop=(n == 1))
                mm.then_inc(bc_full, 1)
            barrier(pe, 1)
            job = JOB["zg"]

            def pe_zg(b, k, last):
                need(out_taken, 1, lag=2)
                pe_products(pe, need, b + job.u0, k, bank[k][:, :], lambda s: hh[:, s, CTX:TOK], lambda s: hl[:, s, CTX:TOK],
                            KB, LAT)

            in_turns(pe, need, job, {out_taken: 2}, pe_zg)
            barrier(pe, 2)

            for n in range(10):
                t, d = n // 2, n % 2
                c = SSEQ[d][t]
                need(xw_ready)
                need(st_taken, 1, lag=2)
                for gr in range(2):
                    mm = pe.matmul(bank[n % 2][64 * gr:64 * gr + 64, :], btm[:, c * P + 64 * gr:c * P + 64 * gr + 64],
                                   xwb[n % 2][:, 512 * gr:512 * gr + 512], start=True, stop=True)
                mm.then_inc(st_full, 1)
            pe.wait_ge(st_taken, 10)
            for ci in range(4):
                c = NCTX + ci
                need(sc_copied, 1, lag=1)
                for gr in range(2):
                    mm = pe.matmul(bank[gr][:, 0:P], bf[64 * gr:64 * gr + 64, c * P:(c + 1) * P],
                                   cfm[64 * gr:64 * gr + 64, ci * P:(ci + 1) * P], start=True, stop=True)
                mm.then_inc(sc_full, 1)
                for m in range(4):
                    d, q = m // 2, m % 2
                    need(cp_ready, 1, lag=2)
                    if q == 0:
                        need(eb_ready)
                    for jj in range(4):
                        for n, e in enumerate(ebc):
                            mm = pe.matmul(bank[2 + m % 2][:, jj * P:(jj + 1) * P], e[:, (4 * q + jj) * P:(4 * q + jj + 1) * P], identr[:, :],
                                           start=(n == 0), stop=(n == 1))
                    mm.then_inc(cp_full, 1)

                def decays(hp):
                    need(l_ready, 1, lag=2)
                    bk = bank[4 + hp % 2]
                    pe.matmul(bk[:, :], cbf(0), b4(cbf(1, 2), 2), start=True, stop=False)
                    for e in range(4):
                        for n, gg in enumerate((ghi, glo)):
                            o = dcol(e % 2, c, 2 * hp + e // 2)
                            mm = pe.matmul(bk[:, e * P:(e + 1) * P], ex(gg[:, o:o + 1], P), identr[:, :], start=False,
                                           stop=(e == 3 and n == 1))
                    mm.then_inc(l_full, 1)

                decays(0)
                decays(1)

                for b in range(KB):
                    if b + 2 < KB:
                        decays(b + 2)
                    gr = b // 4
                    if b == 0:
                        need(cp_ready, 0)
                        need(y_taken, 2, lag=2)
                    need(w_ready)
                    for hh_ in range(2):
                        h = 2 * b + hh_
                        dst = bank[6 + gr][64 * hh_:64 * hh_ + 64, (b % 4) * P:(b % 4 + 1) * P]
                        pe.matmul(dst, xtm[:, c * D + h * 64:c * D + (h + 1) * 64], wmat[:, h * P:(h + 1) * P], start=True, stop=False)
                        for d in range(2):
                            slot = ci if d == 0 else 3 - ci
                            o = (d * 4 + slot) * 512 + (h % 8) * 64
                            mm = pe.matmul(dst, hst[64 * gr:64 * gr + 64, o:o + 64],
                                           cpm[64 * gr:64 * gr + 64, (d * 8 + h % 8) * P:(d * 8 + h % 8 + 1) * P],
                                           start=False, stop=(d == 1))
                    if b % 4 == 3:
                        mm.then_inc(y_full, 1)
            barrier(pe, 3)

            A, B = bank[0:4], bank[4:8]
            for t in range(NCH):
                lat = t >= NCTX
                for q in range(4):
                    c = GSEQ[q // 2][t]
                    if t > NCTX:
                        need(o_added)
                    for j in range(4):
                        h = 4 * (q % 2) + j
                        mm = pe.transpose(A[q][:, j * P:(j + 1) * P], kf[:, h * TOK + c * P:h * TOK + (c + 1) * P], const("ident"))
                    mm.then_inc(ktm_full, 1)
                for q in range(4):
                    d, c = q // 2, GSEQ[q // 2][t]
                    need(s_ready)
                    pe.matmul(B[q][:, :], cbf(0), b4(cbf(1 + d)), start=True, stop=False)
                    for j in range(4):
                        for n, gg in enumerate((ghi, glo)):
                            o = dcol(d, c, SH + 4 * (q % 2) + j)
                            mm = pe.matmul(B[q][:, j * P:(j + 1) * P], ex(gg[:, o:o + 1], P), identr[:, :], start=False,
                                           stop=(j == 3 and n == 1))
                    mm.then_inc(gb_full, 1)
                for q in range(4):
                    c = GSEQ[q // 2][t]
                    need(kd_ready)
                    for j in range(4):
                        h = 4 * (q % 2) + j
                        kc = kf[:, h * TOK + c * P:h * TOK + (c + 1) * P]
                        mm = pe.matmul(A[q][:, j * P:(j + 1) * P], kc, kc, start=True, stop=True)
                    mm.then_inc(gram_full, 1)
                for q in range(4):
                    need(c_ready)
                    need(dec_ready)
                    for j in range(4):
                        mm = pe.transpose(B[q][:, j * P:(j + 1) * P], CS[q][:, j * P:(j + 1) * P], const("ident"))
                    mm.then_inc(c1_full, 1)

                def four(dst, w, x):
                    for j in range(4):
                        o = slice(j * P, (j + 1) * P)
                        mm = pe.matmul(dst[:, o], w[:, o], x[:, o], start=True, stop=True)
                    return mm

                for l in range(1, LEVELS):
                    for q in range(4):
                        need(c_ready)
                        need(d_ready)
                        need(dt_ready)
                        four(A[q], CS[q], Dm[q]).then_inc(p_full, 1)
                    for q in range(4):
                        need(p_ready)
                        if l < LEVELS - 1:
                            four(B[q], DT[q], PM[q]).then_inc(dp_full, 1)
                        four(A[q], PM[q], DT[q]).then_inc(dtp_full, 1)
                if lat:
                    for q in range(4):
                        d, c = q // 2, GSEQ[q // 2][t]
                        for j in range(4):
                            for n, e in enumerate((eghi, eglo)):
                                o = dcol(d, c, SH + 4 * (q % 2) + j)
                                mm = pe.matmul(B[q][:, j * P:(j + 1) * P], ex(e[:, o:o + 1], P), identr[:, :], start=(n == 0), stop=(n == 1))
                        mm.then_inc(egb_full, 1)
                for q in range(4):
                    c = GSEQ[q // 2][t]
                    need(dt_ready)
                    if lat:
                        for j in range(4):
                            h = 4 * (q % 2) + j
                            mm = pe.matmul(A[q][:, j * P:(j + 1) * P], kf[:, h * TOK + c * P:h * TOK + (c + 1) * P],
                                           qf[:, h * LAT + (c - NCTX) * P:h * LAT + (c - NCTX + 1) * P], start=True, stop=True)
                        mm.then_inc(qk_full, 1)
                for q in range(4):
                    c = GSEQ[q // 2][t]
                    if lat:
                        need(qe_ready)
                    for j in range(4):
                        h = 4 * (q % 2) + j
                        mm = pe.matmul(B[q][:, j * P:(j + 1) * P], kf[:, h * TOK + c * P:h * TOK + (c + 1) * P],
                                       S[q][:, j * P:(j + 1) * P], start=True, stop=True)
                    mm.then_inc(ks_full, 1)
                for q in range(4):
                    need(r_ready)
                    if lat:
                        need(qkd_ready)
                    four(A[q], DT[q], RM[q]).then_inc(dr_full, 1)
                for q in range(4):
                    need(vn_ready)
                    if lat:
                        for j in range(4):
                            o = slice(j * P, (j + 1) * P)
                            pe.matmul(A[q][:, o], S[q][:, o], QE[q][:, o], start=True, stop=False)
                            mm = pe.matmul(A[q][:, o], VN[q][:, o], QKD[q][:, o], start=False, stop=True)
                        mm.then_inc(o_full, 1)
                    if t < NCH - 1:
                        four(B[q], KD[q], VN[q]).then_inc(s_full, 1)
            barrier(pe, 4)

            sums = [0]

            def pe_rms(n, w="ones"):
                gi = sums[0]
                sums[0] += 1
                need(rs_ready, 1, lag=2)
                for i in range(n):
                    need(q_ready)
                    pe.matmul(bank[6 + gi % 2][:, :], const(w), sqn(gi, i), start=(i == 0), stop=(i == n - 1)).then_inc(q_used, 1)

            sq_i, sq_set = [0], ["a"]

            def sqn(gi, i):
                s = work[sq_set[0]][0][sq_i[0] % 2]
                sq_i[0] += 1
                return s[:, :]

            def plain(job, rhi, rlo, fresh=False):
                def body(b, k, last):
                    need(out_taken, 1, lag=2)
                    fresh_now = fresh and isinstance(b, int) and b == 0
                    pe_products(pe, need, b + job.u0, k, bank[k][:, :], lambda s: blk(rhi, s), lambda s: blk(rlo, s), job.kc, LAT,
                                each=t_lo if fresh_now else None)
                in_turns(pe, need, job, {out_taken: 2}, body, peel=fresh)

            for i in (*range(KB, 2 * KB), *range(KB)):
                need(q_ready)
                g = i // 4 if i < KB else i - 6
                s = sqn(0, i)
                for c in range(4):
                    o = 4 * g + c
                    dst = bank[6][:, o:o + 1] if i >= KB else bank[c][:, g:g + 1]
                    mm = pe.matmul(dst, s[:, c * P:(c + 1) * P], const("ones")[:, 0:1], start=(i >= KB or i % 4 == 0),
                                   stop=(i >= KB or i % 4 == 3))
                mm.then_inc(q_used, 1)
            need(len_hi_ready)
            need(len_lo_ready)
            for g in range(2 + GH):
                if g >= 2:
                    pe.wait_ge(t_ready, min(4 * (g - 1), 8) + max(g - 3, 0))
                for c in range(4):
                    o = 4 * g + c
                    for n, r in enumerate((mn_hi, mn_lo)):
                        mm = pe.matmul(bank[4 + g % 2][:, c * P:(c + 1) * P], ex(r[:, o:o + 1], P), identr[:, :], start=(n == 0), stop=(n == 1))
                mm.then_inc(bc_full, 1)
            barrier(pe, 5)
            job = JOB["wout"]

            def pe_wout(b, k, last):
                need(out_taken, 1, lag=2)
                for e in range(2):
                    pe_products(pe, need, b * 2 + (job.u0 + e), e, bank[k][:, :], lambda s: blk(yhi, 8 * e + s),
                                lambda s: blk(ylo, 8 * e + s), KB, LAT, start=(e == 0), stop=(e == 1))

            in_turns(pe, need, job, {out_taken: 2}, pe_wout)
            barrier(pe, 6)
            sq_set[0] = "b"
            pe_rms(KB)
            need(t_lo, 16)
            for up, down in mlp_jobs():
                plain(up, xhi, xlo, up.name == "up0")
                plain(down, fhi, flo, True)
            barrier(pe, 7)
            pe_rms(KB)
            barrier(pe, 8)
            for l in range(2):
                p0 = 8 + 4 * l
                pe_rms(KB)
                plain(JOB[f"win{l}"], xhi, xlo, True)
                barrier(pe, p0 + 1)
                pe_rms(3)
                pe_rms(2)
                need(t_lo, 5)
                plain(JOB[f"uq{l}"], chi, clo)
                job = JOB[f"uk{l}"]

                def pe_uk(b, k, last):
                    need(out_taken, 1, lag=2)
                    pe_products(pe, need, b + job.u0, k, bank[k][:, :], lambda s: blk(chi, 3 + s), lambda s: blk(clo, 3 + s), 2, LAT)

                in_turns(pe, need, job, {out_taken: 2}, pe_uk)
                job = JOB[f"uv{l}"]
                pe.wait_ge(hi_ready, job.u0 + 2)
                pe.wait_ge(lo_ready, job.u0 + 2)
                for tb in range(4):
                    for s in range(2):
                        xh = chi[:, (3 + s) * LAT + tb * P:(3 + s) * LAT + (tb + 1) * P]
                        xl = clo[:, (3 + s) * LAT + tb * P:(3 + s) * LAT + (tb + 1) * P]
                        pe.matmul(bank[2 + tb][:, :], xh, whi[s][:, 0:LAT], start=(s == 0), stop=False)
                        pe.matmul(bank[2 + tb][:, :], xh, wlo[s][:, 0:LAT], start=False, stop=False)
                        mm = pe.matmul(bank[2 + tb][:, :], xl, whi[s][:, 0:LAT], start=False, stop=(s == 1))
                mm.then_inc(unit_done, 2)
                barrier(pe, p0 + 2)

                n_att = 4 * MH

                def scores(m):
                    h, qb = m // 4, m % 4
                    need(e_ready, 1, lag=3)
                    pe.matmul(bank[(0, 1, 6)[m % 3]][:, :], qh[:, h * LAT + qb * P:h * LAT + (qb + 1) * P], blk(kh, h), start=True,
                              stop=True).then_inc(s2_full, 1)

                def attend(m):
                    h, qb = m // 4, m % 4
                    need(pt_ready)
                    if m % 8 == 0:
                        need(ao_taken, 1, lag=2)
                    for kb_ in range(4):
                        mm = pe.matmul(bank[4 + (h // 2) % 2][64 * (h % 2):64 * (h % 2) + 64, qb * P:(qb + 1) * P],
                                       vh[:, kb_ * LAT + h * 64:kb_ * LAT + (h + 1) * 64], pt[m % 2][:, kb_ * P:(kb_ + 1) * P],
                                       start=(kb_ == 0), stop=(kb_ == 3))
                    mm.then_inc(pv_done, 1)

                scores(0)
                scores(1)
                for m in range(n_att):
                    if m + 2 < n_att:
                        scores(m + 2)
                    need(pn_ready)
                    for kb_ in range(4):
                        mm = pe.transpose(bank[2 + m % 2][:, kb_ * P:(kb_ + 1) * P], eb[m % 3][:, kb_ * P:(kb_ + 1) * P], const("ident"))
                    mm.then_inc(tp_full, 1)
                    if m >= 1:
                        attend(m - 1)
                attend(n_att - 1)
                for b in range(2):
                    need(pd_ready)
                    for e in range(2):
                        r = slice(64 * e, 64 * e + 64)
                        mm = pe.matmul(bank[b][r, :], wpb[r, b * 64:(b + 1) * 64], px[b][r, 0:LAT], start=True, stop=True)
                    mm.then_inc(pw_full, 1)
                for b in range(2):
                    pe_rms(1, "half")
                need(vn2_ready, 2)
                for b in range(2):
                    for cc in range(4):
                        mm = pe.transpose(bank[2 + b][:, cc * P:(cc + 1) * P], pf[:, (10 + b) * LAT + cc * P:(10 + b) * LAT + (cc + 1) * P], const("ident"))
                    mm.then_inc(vt2_full, 1)
                for b in range(2):
                    need(vt2_ready)
                    for e in range(2):
                        for cc in range(4):
                            gx = 2 * b + e
                            mm = pe.matmul(bank[4 + b][64 * e:64 * e + 64, cc * P:(cc + 1) * P],
                                           vts[:, (4 * b + cc) * P + 64 * e:(4 * b + cc) * P + 64 * e + 64], wsb[:, gx * P:(gx + 1) * P],
                                           start=True, stop=True)
                    mm.then_inc(sg_full, 1)
                barrier(pe, p0 + 3)
                need.skip(t_lo, 2)
                plain(JOB[f"wo{l}"], xhi, xlo)
                barrier(pe, p0 + 4)
                pe_rms(KB)
                for j, (gu, dn) in enumerate(ffn_jobs(l)):
                    plain(gu, xhi, xlo, j == 0)
                    plain(dn, fhi, flo, True)
            pe_rms(KB)
            barrier(pe, 17)

        @block.scalar
        def _(act):
            need = Need(act)
            need(const_loaded, 48)
            act.activation(cs[:, :], vc("c"), ACT.Silu).then_inc(cs_ready, 1)

            def act_norm(need, x, n, parts, scale, sqs, rt):
                for b in range(n):
                    need(sq_used, 1, lag=2)
                    src = x(b)
                    act.activation(sqs[b % 2][:, parts[0][1]:parts[-1][2]], src, ACT.Square).then_inc(sq_ready, 1)
                need.seen[sq_used.name] = need.seen.get(sq_used.name, 0)
                act.wait_ge(sq_used, need.seen[sq_used.name])
                for bk, lo, hi in parts:
                    act.activation(rt[:, lo:hi], bk[:, 0:hi - lo], ACT.Sqrt, bias=EPS, scale=scale).then_inc(root_ready, 1)

            need(x_loaded, 16)
            act_norm(need, lambda b: v3(xt, KB)[:, b, :], KB, [(bank[5], 0, CTX), (bank[4], CTX, TOK)], 1.0 / D, sq, root)
            for b in range(KB):
                need(scaled, 2)
                for lo, hi, m in ((0, CTX, 1), (CTX, TOK, 0)):
                    act.activation(hhi[:, b * TOK + lo:b * TOK + hi], tmp[b % 2][:, lo:hi], ACT.Identity,
                                   bias=modv[:, 2 * b + m:2 * b + m + 1]).then_inc(hi_out, 1)
            need(small_loaded, 16)
            act.activation(wsmhi[:, :], wsm[:, :], ACT.Identity).then_inc(smallw_hi, 1)

            job = JOB["qkvx"]
            split_hi(act, 0, 0, KB)
            need(pads_ready)

            def silu(u):
                act.wait_ge(conv_done, u + 1)
                if 8 <= u < 24:
                    need(tm_full, 1, lag=1)
                c = cacc[u % 2]
                if u < 8:
                    dst = kf[:, u * TOK:(u + 1) * TOK]
                elif u < 24:
                    dst = sil
                elif u == 24:
                    dst = bf
                else:
                    dst = None
                if dst is not None:
                    act.activation(dst[:, 0:CTX], c[:, 0:CTX], ACT.Silu, bias=vc("convb", u, 1)).then_inc(sil_ready, 1)
                    lat = dst[:, CTX:TOK]
                else:
                    lat = cfm[:, :] if u == 25 else qf[:, (u - 26) * LAT:(u - 25) * LAT]
                act.activation(lat.rearrange("p (r c) -> p r c", r=8), rows(c, CTX + 2), ACT.Silu,
                               bias=vc("convb", u, 1)).then_inc(sil_ready, 1)

            def token_major(u):
                act.wait_ge(tm_full, u - 7)
                dst, n = (vt, u - 8) if u < 16 else (xtm, u - 16) if u < 24 else (btm, 0)
                dv = v3(dst, NCH)
                act.activation(dv[:, 0:4, n * P:(n + 1) * P], bank[4][:, :].rearrange("p (c t) -> p c t", c=4),
                               ACT.Identity).then_inc(tm_taken, 1)
                act.activation(dv[:, 4:6, n * P:(n + 1) * P], bank[5][:, 0:2 * P].rearrange("p (c t) -> p c t", c=2),
                               ACT.Identity).then_inc(tm_taken, 1)

            for u in range(job.n + 2):
                if u < job.n:
                    split_hi(act, u + 1, (u + 1) % 2, KB)
                    act.wait_ge(unit_done, u + 1)
                    if u >= 2:
                        act.wait_ge(conv_done, u - 1)
                    if has_ctx(u):
                        act.activation(cbuf[u % 2][:, 2:2 + CTX], bank[2 + u % 2][:, 0:CTX], ACT.Identity).then_inc(cb_ready, 1)
                    act.activation(rows(cbuf[u % 2], CTX + 4), bank[u % 2][:, :].rearrange("p (r c) -> p r c", r=8),
                                   ACT.Identity).then_inc(cb_ready, 1)
                if 1 <= u <= job.n:
                    silu(u - 1)
                if 8 <= u - 2 < 25:
                    token_major(u - 2)
                if u == 0:
                    act.activation(ea[:, :], vc("alog"), ACT.Exp).then_inc(act_done, 1)
                    need(small_dve)
                    act.activation(ee[:, :], ab[:, :], ACT.Exp, scale=-1.0).then_inc(act_done, 1)
                    act.wait_ge(act_done, 2)
                    act.activation(ab[:, :], ee[:, :], ACT.Ln, bias=1.0).then_inc(small_ln, 1)
                    act.activation(beta[:, :].rearrange("p (c x) -> p c x", c=NCH),
                                   bank[6][:, 0:384].rearrange("p (c x) -> p c x", c=NCH)[:, :, 48:64], ACT.Sigmoid).then_inc(small_ln, 1)

            need(cum_full)
            act.wait_ge(act_done, 2)
            act.activation(eg[:, :], bank[6][:, 0:288], ACT.Exp).then_inc(act_done, 1)
            act.activation(er[:, :], bank[0][:, 0:288], ACT.Exp).then_inc(act_done, 1)
            act.activation(et[:, :], bank[1][:, 0:288], ACT.Exp).then_inc(act_done, 1)
            act.activation(ghi[:, :], bank[6][:, 0:288], ACT.Identity).then_inc(act_done, 1)
            act.wait_ge(act_done, 6)
            act.activation(eghi[:, :], eg[:, :], ACT.Identity).then_inc(act_done, 1)
            need(small_dve)
            act.activation(lndt[:, :], lndt[:, :], ACT.Ln).then_inc(small_ln, 1)
            act.wait_ge(conv_done, job.n)
            act.wait_ge(sil_ready, conv_ops(job.n))

            def square(h):
                if h >= 2:
                    act.wait_ge(sum_full, h - 1)
                src, lo = (kf[:, h * TOK:(h + 1) * TOK], 0) if h < GH else (qf[:, (h - GH) * LAT:(h - GH + 1) * LAT], CTX)
                act.activation(sq2[h % 2][:, lo:TOK], src, ACT.Square).then_inc(sq_ready, 1)

            for h in range(2 * GH):
                square(h)
            act.wait_ge(sum_full, 2 * GH)
            nk = GH * NCH
            act.activation(len_root[:, 0:nk], bank[2][:, 0:nk], ACT.Sqrt, bias=EPS)
            act.activation(len_root[:, nk:NLEN], bank[2][:, nk:NLEN], ACT.Sqrt, bias=EPS * GK, scale=float(GK)).then_inc(len_rooted, 1)
            need(len_inverse)
            act.activation(len_hi[:, :], len_rs[:, :], ACT.Identity).then_inc(len_hi_ready, 1)
            barrier(act, 1)
            job = JOB["zg"]

            def act_zg(b, k, last):
                split_next(split_hi, act, job, b, k, last)
                act.wait_ge(unit_done, b + (job.u0 + 1))
                if not isinstance(b, int) or b >= 2:
                    act.wait_ge(zg_stored[k], b * 8 - 8 * k)
                act.activation(stg[k][:, :], bank[k][:, :], ACT.Silu).then_inc(out_taken, 1)
                act.wait_ge(out_taken, b + 1)
                dst = zg_dram[b] if isinstance(b, int) else zg_dram[bass.ds(b, 1)].rearrange("o p n -> (o p) n")
                act.dma_start(dst, stg[k][:, :]).then_inc(zg_stored[k], 16)

            in_turns(act, need, job, {}, act_zg)
            for k in range(2):
                act.wait_ge(zg_stored[k], 8 * job.n)
            barrier(act, 2)

            for ci in range(4):
                c = NCTX + ci
                need(sc_full)
                if ci:
                    act.wait_ge(w_ready, KB * ci)
                for gr in range(2):
                    cp_ = act.activation(stb[:, gr * P:(gr + 1) * P], bank[gr][:, 0:P], ACT.Identity)
                cp_.then_inc(sc_copied, 1)
                for hp in range(KB):
                    need(l_full)
                    need(w_ready, 1, lag=2)
                    for e in range(4):
                        o = dcol(e % 2, c, 2 * hp + e // 2)
                        ins = act.activation(lbuf[hp % 2][:, e * P:(e + 1) * P], bank[4 + hp % 2][:, e * P:(e + 1) * P], ACT.Exp,
                                             bias=ng[:, o:o + 1])
                    ins.then_inc(l_ready, 1)
                    if hp == 5 or hp == 7:
                        gr = int(hp == 7)
                        need(y_full)
                        act.activation(v3(yfm, KB)[:, 4 * gr:4 * gr + 4, ci * P:(ci + 1) * P], h4(bank[6 + gr][:, :]),
                                       ACT.Identity).then_inc(y_taken, 1)
            barrier(act, 3)

            act.dma_start(y_dram, yfm[:, :]).then_inc(y_spilled, 16)
            A, B = bank[0:4], bank[4:8]
            for t in range(NCH):
                for q in range(4):
                    d, c = q // 2, GSEQ[q // 2][t]
                    need(gb_full)
                    for j in range(4):
                        o = dcol(d, c, SH + 4 * (q % 2) + j)
                        ins = act.activation(DEC[q][:, j * P:(j + 1) * P], B[q][:, j * P:(j + 1) * P], ACT.Exp, bias=ng[:, o:o + 1])
                    ins.then_inc(dec_ready, 1)
                for l in range(1, LEVELS):
                    for q in range(4):
                        need(p_full)
                        act.activation(PM[q][:, :], A[q][:, :], ACT.Identity).then_inc(p_ready, 1)
                for q in range(4):
                    d, c = q // 2, GSEQ[q // 2][t]
                    need(dr_full)
                    for j in range(4):
                        o = c * 16 + d * 8 + 4 * (q % 2) + j
                        ins = act.activation(VN[q][:, j * P:(j + 1) * P], A[q][:, j * P:(j + 1) * P], ACT.Identity, scale=beta[:, o:o + 1])
                    ins.then_inc(vn_ready, 1)
            barrier(act, 4)

            q_n, g_n, t_n, sets = [0], [0], [0], ["a"]

            def act_rms(srcs, n_feat, eps=EPS):
                sqs, rss = work[sets[0]][0:2]
                for s in srcs:
                    if q_n[0] >= 2:
                        act.wait_ge(q_used, q_n[0] - 1)
                    act.activation(sqs[q_n[0] % 2][:, :], s, ACT.Square).then_inc(q_ready, 1)
                    q_n[0] += 1
                act.wait_ge(q_used, q_n[0])
                gi = g_n[0]
                g_n[0] += 1
                if gi:
                    act.wait_ge(rs_ready, gi)
                act.activation(lnb[:, :], bank[6 + gi % 2][:, :], ACT.Ln, bias=eps, scale=1.0 / n_feat).then_inc(ln_done, 1)
                act.wait_ge(ln_done, gi + 1)
                if gi >= 2:
                    act.wait_ge(rs_used, gi - 1)
                act.activation(rss[gi % 2][:, :], lnb[:, :], ACT.Exp, scale=-0.5).then_inc(rs_ready, 1)

            def act_hi(dsts, bias=None):
                tps = work[sets[0]][2]
                for i, dst in enumerate(dsts):
                    need(t_ready)
                    b = 0.0 if bias is None else bias(i)
                    act.activation(dst, tps[t_n[0] % 2][:, :], ACT.Identity, bias=b).then_inc(t_hi, 1)
                    t_n[0] += 1

            act.dma_start(cntb[:, :], a["cnt"]).then_inc(tab_loaded, 16)
            act.dma_start(posb[:, :], a["pos"]).then_inc(tab_loaded, 16)
            act.dma_start(v3(zb, KB), zg_dram[0:KB].rearrange("b p n -> p b n")).then_inc(back_loaded, 16)
            act.dma_start(v3(gateb, KB), zg_dram[KB:2 * KB].rearrange("b p n -> p b n")).then_inc(back_loaded, 16)
            act.dma_start(yb[:, :], y_dram).then_inc(back_loaded, 16)
            act.dma_start(v3(xr, KB), a["xt"].rearrange("p (b t) -> p b t", b=KB)[:, :, CTX:TOK]).then_inc(xr_loaded, 16)
            def square_for(src):
                if q_n[0] >= 2:
                    act.wait_ge(q_used, q_n[0] - 1)
                act.activation(work[sets[0]][0][q_n[0] % 2][:, :], src, ACT.Square).then_inc(q_ready, 1)
                q_n[0] += 1

            for i in (*range(KB, 2 * KB), *range(KB)):
                if i < KB:
                    need(v_ready)
                square_for(blk(yb, i) if i < KB else blk(ofm, i - KB))
            act.wait_ge(q_used, q_n[0])
            for c in range(4):
                act.activation(mn_root[:, 0:8].rearrange("p (g c) -> p g c", g=2)[:, :, c], bank[c][:, 0:2], ACT.Sqrt, bias=EPS, scale=1.0 / 512)
            act.activation(mn_root[:, 8:MN_], bank[6][:, 8:MN_], ACT.Sqrt, bias=EPS, scale=1.0 / GK).then_inc(len_rooted, 1)
            need(len_inverse)
            act.activation(mn_hi[:, :], mn_rs[:, :], ACT.Identity).then_inc(len_hi_ready, 1)
            need(rope_step)
            act.activation(rb[:, :], ra[:, :], ACT.Sin).then_inc(rope_sin, 1)
            act_hi([blk(yhi, b) for b in range(2 * KB)])
            barrier(act, 5)
            job = JOB["wout"]

            def act_wout(b, k, last):
                split_hi(act, b * 2 + (job.u0 + 1), 1, KB)
                split_hi(act, b * 2 + (job.u0 + 2), 0, KB)

            in_turns(act, need, job, {}, act_wout)
            barrier(act, 6)

            def act_plain(job, evac=None):
                def body(b, k, last):
                    split_next(split_hi, act, job, b, k, last)
                    if evac:
                        evac(job, b, k)
                in_turns(act, need, job, {}, body)

            def act_up(job):
                def body(b, k, last):
                    split_next(split_hi, act, job, b, k, last)
                    act.wait_ge(unit_done, b + (job.u0 + 1))
                    act.wait_ge(out_taken, b + (job.b0 - JOB["zg"].b0 - 1))
                    act.activation(rt[k][:, :], bank[k][:, :], ACT.Relu).then_inc(relu_ready, 1)
                    need(t_ready)
                    act.activation(blk(fhi, b), work["b"][2][k][:, :], ACT.Identity).then_inc(t_hi, 1)
                in_turns(act, need, job, {t_ready: 2}, body)
                t_n[0] += job.n

            sets[0] = "b"
            act_rms([blk(xr, b) for b in range(KB)], D)
            act_hi([blk(xhi, b) for b in range(KB)], lambda b: aff[:, 32 + b:33 + b])
            for up, down in mlp_jobs():
                act_up(up)
                act_plain(down)
            barrier(act, 7)
            act_rms([blk(xr, b) for b in range(KB)], D)
            barrier(act, 8)
            for l in range(2):
                p0 = 8 + 4 * l
                if l:
                    act.wait_ge(out_taken, JOB["dn02"].b0 - JOB["zg"].b0 + 8)
                act_rms([blk(xr, b) for b in range(KB)], D)
                act_hi([blk(xhi, b) for b in range(KB)])
                job = JOB[f"win{l}"]

                def act_win(job, b, k):
                    act.wait_ge(unit_done, b + (job.u0 + 1))
                    act.activation(blk(pf, b), bank[k][:, :], ACT.Identity).then_inc(out_taken, 1)

                act_plain(job, act_win)
                act.dma_start(wpb[:, :], a["wpool"][l]).then_inc(tab_loaded, 16)
                act.dma_start(wsb[:, :], a["ws"][l]).then_inc(tab_loaded, 16)
                act.dma_start(bsb[:, :], a["bs"][l]).then_inc(tab_loaded, 16)
                barrier(act, p0 + 1)
                act_rms([blk(pf, i) for i in range(3)], QR)
                act_hi([blk(chi, i) for i in range(3)])
                act_rms([blk(pf, 3 + i) for i in range(2)], KVR)
                act_hi([blk(chi, 3 + i) for i in range(2)])

                def act_uq(job, b, k):
                    act.wait_ge(unit_done, b + (job.u0 + 1))
                    act.activation(blk(qh, b)[64:P, :], bank[k][64:P, :], ACT.Identity, scale=QS).then_inc(act_part, 1)

                act_plain(JOB[f"uq{l}"], act_uq)

                def act_uk(job, b, k):
                    act.wait_ge(unit_done, b + (job.u0 + 1))
                    act.activation(kh[64:P, b * 2 * LAT:(b * 2 + 1) * LAT] if isinstance(b, int) else kh[64:P, bass.ds(b * 1024, LAT)],
                                   bank[k][0:64, :], ACT.Identity)
                    act.activation(kh[64:P, (b * 2 + 1) * LAT:(b * 2 + 2) * LAT] if isinstance(b, int) else kh[64:P, bass.ds(b * 1024 + LAT, LAT)],
                                   bank[k][64:P, :], ACT.Identity).then_inc(out_taken, 1)

                act_plain(JOB[f"uk{l}"], act_uk)
                job = JOB[f"uv{l}"]
                split_hi(act, job.u0 + 1, 1, 4)
                act.wait_ge(unit_done, job.u0 + 2)
                for tb in range(4):
                    ins = act.activation(blk(vh, tb), bank[2 + tb][:, :], ACT.Identity)
                ins.then_inc(uv_taken, 1)
                split_hi(act, job.u0 + 2, 0, job.next_kc)
                barrier(act, p0 + 2)

                n_att = 4 * MH

                def copy_pt(m):
                    need(tp_full)
                    if m + n_att * l >= 2:
                        act.wait_ge(pv_done, m + n_att * l - 1)
                    act.activation(pt[m % 2][:, :], bank[2 + m % 2][:, :], ACT.Identity).then_inc(pt_ready, 1)

                def out_hi(m):
                    act.wait_ge(pv_done, m + n_att * l + 1)
                    hp = m // 8
                    act.activation(blk(xhi, hp), bank[4 + hp % 2][:, :], ACT.Identity).then_inc(ao_hi, 1)

                for m in range(n_att):
                    need(mx_ready)
                    if m >= 3:
                        act.wait_ge(tp_full, m + n_att * l - 2)
                    act.activation(eb[m % 3][:, :], bank[(0, 1, 6)[m % 3]][:, :], ACT.Exp, bias=smal[:, m % 3:m % 3 + 1],
                                   accum_out=smal[:, 3 + m % 3:4 + m % 3]).then_inc(e_ready, 1)
                    if m >= 2:
                        copy_pt(m - 2)
                    if m >= 3 and (m - 3) % 8 == 7:
                        out_hi(m - 3)
                copy_pt(n_att - 2)
                copy_pt(n_att - 1)
                out_hi(n_att - 1)
                for b in range(2):
                    need(pw_full)
                    act.activation(blk(xhi, 4 + b), bank[b][:, :], ACT.Identity, scale=vc(f"psc{l}", b, 1)).then_inc(pw_hi, 1)
                for b in range(4):
                    act.activation(blk(pf, 8 + b), blk(pf, 8 + b), ACT.Gelu_apprx_tanh).then_inc(gelu_ready, 1)
                act.wait_ge(gelu_ready, 4 * l + 4)
                for b in range(2):
                    act_rms([blk(pf, 10 + b)], 64)
                for b in range(2):
                    need(vt2_full)
                    act.activation(vts[:, 4 * b * P:4 * (b + 1) * P], bank[2 + b][:, :], ACT.Identity).then_inc(vt2_ready, 1)
                act_hi([blk(xhi, 6 + b) for b in range(2)])
                barrier(act, p0 + 3)
                act_plain(JOB[f"wo{l}"])
                barrier(act, p0 + 4)
                act_rms([blk(xr, b) for b in range(KB)], D)
                act_hi([blk(xhi, b) for b in range(KB)])

                def act_gu(job):
                    def body(b, k, last):
                        split_next(split_hi, act, job, b, k, last)
                        if k == 0:
                            act.wait_ge(unit_done, b + (job.u0 + 1))
                            act.wait_ge(out_taken, b + (job.b0 - JOB["zg"].b0))
                            act.activation(rt[0][:, :], bank[0][:, :], ACT.Silu).then_inc(out_taken, 1)
                            return
                        act.wait_ge(out_taken, b + (job.b0 - JOB["zg"].b0 + 1))
                        dst = blk(fhi, b // 2) if isinstance(b, int) else fhi[:, bass.ds(b * 256 - 256, LAT)]
                        act.activation(dst, work["b"][2][0][:, :], ACT.Identity).then_inc(t_hi, 1)
                    in_turns(act, need, job, {}, body)
                    need.skip(t_ready, job.n // 2)
                    t_n[0] += job.n // 2

                for gu, dn in ffn_jobs(l):
                    act_gu(gu)
                    act_plain(dn)
            act.wait_ge(out_taken, JOB["dn12"].b0 - JOB["zg"].b0 + 8)
            act_rms([blk(xr, b) for b in range(KB)], D)
            barrier(act, 17)
            act.dma_start(out.rearrange("(b p) t -> p b t", p=P), v3(xr, KB)).then_inc(out_stored, 16)
            act.wait_ge(out_stored, 16)

        @block.vector
        def _(dve):
            need = Need(dve)
            marked = [0]

            def after(ins):
                marked[0] += 1
                ins.then_inc(dve_done, 1)
                dve.wait_ge(dve_done, marked[0])

            need(const_loaded, 48)
            dve.tensor_copy(identr[:, :], const("ident")).then_inc(identr_ready, 1)

            def modulation(lo, hi):
                need(mod_done, hi - lo)
                after(dve.tensor_tensor(modv[:, 2 * lo:2 * hi].rearrange("p (u m) -> p u m", m=2), bank[7][:, 2 * lo:2 * hi].rearrange("p (u m) -> p u m", m=2),
                                        vc("b_mod", lo, hi - lo).unsqueeze(2).broadcast_to((P, hi - lo, 2)), ALU.add))
                mv = modv[:, :].rearrange("p (c b m) -> p c b m", c=6, m=2)
                gains = ((mv[:, 1, :, 0], "norm1"), (mv[:, 1, :, 1], "norm1"), (mv[:, 4, :, 0], "norm2"))
                for n in (0, 1) if lo == 0 else (2,):
                    src, gain = gains[n]
                    after(dve.scalar_tensor_tensor(out=aff[:, 8 * n:8 * n + 8], in0=src, scalar=1.0, in1=vc(gain), op0=ALU.add, op1=ALU.mult))
                if lo:
                    for n, c in enumerate((2, 3, 5)):
                        after(dve.tensor_copy(aff[:, 24 + 8 * n:32 + 8 * n], mv[:, c, :, 0]))

            def dve_rstd(need, rt, rs, parts):
                for lo, hi in parts:
                    need(root_ready)
                    after(dve.reciprocal(rs[:, lo:hi], rt[:, lo:hi]))

            dve_rstd(need, root, rstd, ((0, CTX), (CTX, TOK)))
            modulation(0, 16)
            xv = v3(xt, KB)
            for b in range(KB + 1):
                if b < KB:
                    for lo, hi, m in ((0, CTX, 1), (CTX, TOK, 0)):
                        if b >= 2:
                            dve.wait_ge(lo_out, 2 * (b - 1))
                        dve.scalar_tensor_tensor(out=tmp[b % 2][:, lo:hi], in0=xv[:, b, lo:hi], scalar=aff[:, 8 * m + b:8 * m + b + 1],
                                                 in1=rstd[:, lo:hi], op0=ALU.mult, op1=ALU.mult).then_inc(scaled, 1)
                if b >= 1:
                    c = b - 1
                    need(hi_out, 2)
                    dve.wait_ge(scaled, 2 * c + 2)
                    for lo, hi, m in ((0, CTX, 1), (CTX, TOK, 0)):
                        dve.scalar_tensor_tensor(out=hlo[:, c * TOK + lo:c * TOK + hi], in0=tmp[c % 2][:, lo:hi],
                                                 scalar=modv[:, 2 * c + m:2 * c + m + 1], in1=hhi[:, c * TOK + lo:c * TOK + hi].bitcast(F32),
                                                 op0=ALU.add, op1=ALU.subtract).then_inc(lo_out, 1)
            need(smallw_hi)
            dve.tensor_tensor(wsmlo[:, :], wsm[:, :], wsmhi[:, :].bitcast(F32), ALU.subtract).then_inc(smallw_ready, 1)

            job = JOB["qkvx"]
            split_lo(dve, 0, 0, KB)

            def conv(u):
                dve.wait_ge(cb_ready, conv_ops(u + 1))
                if u >= 2:
                    dve.wait_ge(sil_ready, conv_ops(u - 1))
                lo = 0 if has_ctx(u) else CTX + 2
                acc, src = cacc[u % 2][:, lo:CONVW - 4], cbuf[u % 2]
                for k in range(TAPS):
                    x, w = src[:, lo + k:CONVW - 4 + k], vc("convw", u * TAPS + k, 1)
                    if k == 0:
                        after(dve.tensor_scalar(acc, x, w, None, ALU.mult))
                    elif k < TAPS - 1:
                        after(dve.scalar_tensor_tensor(out=acc, in0=x, scalar=w, in1=acc, op0=ALU.mult, op1=ALU.add))
                    else:
                        dve.scalar_tensor_tensor(out=acc, in0=x, scalar=w, in1=acc, op0=ALU.mult, op1=ALU.add).then_inc(conv_done, 1)

            for u in range(job.n):
                split_lo(dve, u + 1, (u + 1) % 2, KB)
                if u == 0:
                    need(small_full)
                    x48 = bank[6][:, 0:384].rearrange("p (c x) -> p c x", c=NCH)[:, :, 0:48]
                    t3 = lambda t: t[:, :].rearrange("p (c x) -> p c x", c=NCH)
                    bc = lambda v: v.unsqueeze(1).broadcast_to((P, NCH, 48))
                    after(dve.tensor_tensor(t3(xb), x48, bc(vc("bias")), ALU.add))
                    dve.scalar_tensor_tensor(out=ab[:, :], in0=xb[:, :], scalar=-1.0, in1=xb[:, :], op0=ALU.mult, op1=ALU.max).then_inc(small_dve, 1)
                    need(small_ln, 2)
                    after(dve.scalar_tensor_tensor(out=sp[:, :], in0=xb[:, :], scalar=0.0, in1=ab[:, :], op0=ALU.max, op1=ALU.add))
                    dve.scalar_tensor_tensor(out=t3(ga), in0=t3(sp), scalar=-1.0, in1=bc(ea[:, :]), op0=ALU.mult,
                                             op1=ALU.mult).then_inc(small_act, 1)
                conv(u)

            dve.wait_ge(sil_ready, conv_ops(job.n))
            dve.tensor_scalar(lndt[:, :], sp[:, :], 1e-37, None, ALU.max).then_inc(small_dve, 1)
            need(cum_full)
            dve.wait_ge(act_done, 6)
            after(dve.tensor_copy(g[:, :], bank[6][:, 0:288]))
            after(dve.tensor_scalar(ng[:, :], g[:, :], -1.0, None, ALU.mult))
            after(dve.tensor_tensor(glo[:, :], g[:, :], ghi[:, :].bitcast(F32), ALU.subtract))
            dve.wait_ge(act_done, 7)
            after(dve.tensor_tensor(eglo[:, :], eg[:, :], eghi[:, :].bitcast(F32), ALU.subtract))
            d4 = lambda t: t[:, :].rearrange("p (d c x) -> p d c x", d=2, c=NCH)
            for d in range(2):
                spd = sp[:, :].rearrange("p (c x) -> p c x", c=NCH)[:, :, d * NH:(d + 1) * NH]
                after(dve.tensor_tensor(d4(xw)[:, d], spd, d4(er)[:, d], ALU.mult))
            need(small_ln)
            for d in range(2):
                part = d4(ng)[:, d, :, 0:SH]
                after(dve.tensor_tensor(part, part, lndt[:, :].rearrange("p (c x) -> p c x", c=NCH)[:, :, d * NH:d * NH + SH], ALU.add))
            modulation(16, 48)
            need(len_rooted)
            dve.reciprocal(len_rs[:, :], len_root[:, :]).then_inc(len_inverse, 1)
            need(len_hi_ready)
            dve.wait_ge(len_inverse, 1)
            dve.tensor_tensor(len_lo[:, :], len_rs[:, :], len_hi[:, :].bitcast(F32), ALU.subtract).then_inc(len_lo_ready, 1)
            for h in range(2 * GH):
                need(bc_full)
                if h < GH:
                    k = kf[:, h * TOK:h * TOK + CTX]
                    dve.tensor_tensor(k, k, bank[h % 2][:, 0:CTX], ALU.mult)
                lat = kf[:, h * TOK + CTX:(h + 1) * TOK] if h < GH else qf[:, (h - GH) * LAT:(h - GH + 1) * LAT]
                dve.tensor_tensor(lat, lat, bank[4 + h % 2][:, :], ALU.mult).then_inc(bc_used, 1)
            barrier(dve, 1)
            job = JOB["zg"]
            in_turns(dve, need, job, {}, lambda b, k, last: split_next(split_lo, dve, job, b, k, last))
            barrier(dve, 2)

            ev = et[:, :].rearrange("p (x h) -> p x h", h=NH)
            for gr in range(2):
                after(dve.tensor_copy(etb[64 * gr:64 * gr + 64, :].rearrange("p (x h) -> p x h", h=8),
                                      ev[64 * gr:64 * gr + 64, :, 8 * gr:8 * gr + 8]))
            for n in range(11):
                if n < 10:
                    d, c = n % 2, SSEQ[n % 2][n // 2]
                    need(st_full, 0 if n < 2 else 1)
                    dve.tensor_tensor(xwb[n % 2][:, :].rearrange("p (h e) -> p h e", h=SH), xtm[:, c * D:(c + 1) * D].rearrange("p (h e) -> p h e", h=SH),
                                      scal4(xw[:, dcol(d, c):dcol(d, c) + SH], 64), ALU.mult).then_inc(xw_ready, 1)
                if n >= 1:
                    m = n - 1
                    t, d = m // 2, m % 2
                    c = SSEQ[d][t]
                    dve.wait_ge(st_full, m + 1)
                    slot = lambda t: hst[:, (d * 4 + (t - 1) % 4) * 512:(d * 4 + (t - 1) % 4 + 1) * 512]
                    if t == 0:
                        dve.tensor_copy(slot(0), bank[m % 2][:, :]).then_inc(st_taken, 1)
                    else:
                        dve.wait_ge(st_taken, m)
                        after(dve.tensor_tensor(htmp[:, :].rearrange("p (h e) -> p h e", h=8), slot(t - 1).rearrange("p (h e) -> p h e", h=8),
                                                scal4(etb[:, (d * NCH + c) * 8:(d * NCH + c) * 8 + 8], 64), ALU.mult))
                        dve.tensor_tensor(slot(t), htmp[:, :], bank[m % 2][:, :], ALU.add).then_inc(st_taken, 1)
            for ci in range(4):
                c = NCTX + ci
                for m in range(4):
                    d, q = m // 2, m % 2
                    if q == 0:
                        for src, dst in ((eghi, ebc[0]), (eglo, ebc[1])):
                            cols = src[:, dcol(d, c):dcol(d, c) + 16].bitcast(F32).rearrange("p (g j) -> p j g", g=2)
                            ins = dve.tensor_copy(dst[:, :].rearrange("p (j g e) -> p j g e", g=2, e=64),
                                                  cols.unsqueeze(3).broadcast_to((P, 8, 2, 64)))
                        ins.then_inc(eb_ready, 1)
                    need(cp_full)
                    dve.tensor_tensor(h4(cpm[:, (d * 8 + 4 * q) * P:(d * 8 + 4 * q + 4) * P]), h4(bank[2 + m % 2][:, :]),
                                      b4(cfm[:, ci * P:(ci + 1) * P]), ALU.mult).then_inc(cp_ready, 1)
                need(sc_copied)
                for hp in range(KB):
                    need(l_ready)
                    w2 = h4(wmat[:, 2 * hp * P:(2 * hp + 2) * P], 2)
                    gr = hp // 4
                    pair = lbuf[hp % 2][:, :].rearrange("p (e d t) -> p e d t", e=2, d=2)
                    after(dve.tensor_tensor(w2, pair[:, :, 0], pair[:, :, 1], ALU.add))
                    after(dve.tensor_tensor(w2, w2, b4(stb[:, gr * P:(gr + 1) * P], 2), ALU.mult))
                    for e in range(2):
                        h = 2 * hp + e
                        w = wmat[:, h * P:(h + 1) * P]
                        ins = dve.scalar_tensor_tensor(out=w, in0=const("ident"), scalar=vc("ssdD", h, 1), in1=w, op0=ALU.mult, op1=ALU.add)
                    ins.then_inc(w_ready, 1)
            barrier(dve, 3)

            A, B = bank[0:4], bank[4:8]
            after(dve.tensor_scalar(neg_eg[:, :], eg[:, :], -1.0, None, ALU.mult))
            for q in range(4):
                dve.memset(S[q][:, :], 0.0).then_inc(s_ready, 1)
            for t in range(NCH):
                lat = t >= NCTX
                for q in range(4):
                    d, c = q // 2, GSEQ[q // 2][t]
                    need(ktm_full)
                    o = dcol(d, c, SH + 4 * (q % 2))
                    dve.tensor_tensor(h4(KD[q][:, :]), h4(A[q][:, :]), scal4(er[:, o:o + 4], P), ALU.mult).then_inc(kd_ready, 1)
                for q in range(4):
                    d, c = q // 2, GSEQ[q // 2][t]
                    need(gram_full)
                    need(dec_ready)
                    for j in range(4):
                        o, s = c * 16 + d * 8 + 4 * (q % 2) + j, slice(j * P, (j + 1) * P)
                        ins = dve.scalar_tensor_tensor(out=AT[q][:, s], in0=A[q][:, s], scalar=beta[:, o:o + 1], in1=DEC[q][:, s],
                                                       op0=ALU.mult, op1=ALU.mult)
                    ins.then_inc(at_ready, 1)
                for q in range(4):
                    need(c_ready)
                    dve.tensor_tensor(h4(DT[q][:, :]), b4(const("ident")), h4(CS[q][:, :]), ALU.subtract).then_inc(dt_ready, 1)
                need.skip(c_ready, 4 * (LEVELS - 1))
                for q in range(4):
                    need(c1_full)
                    dve.tensor_tensor(h4(Dm[q][:, :]), b4(const("ident")), h4(B[q][:, :]), ALU.subtract).then_inc(d_ready, 1)
                for l in range(1, LEVELS):
                    for q in range(4):
                        if l < LEVELS - 1:
                            need(dp_full)
                            dve.tensor_tensor(Dm[q][:, :], Dm[q][:, :], B[q][:, :], ALU.subtract).then_inc(d_ready, 1)
                        need(dtp_full)
                        dve.tensor_tensor(DT[q][:, :], DT[q][:, :], A[q][:, :], ALU.subtract).then_inc(dt_ready, 1)
                if lat:
                    for q in range(4):
                        c = GSEQ[q // 2][t]
                        need(egb_full)
                        qs = v3(qf, GH)[:, 4 * (q % 2):4 * (q % 2) + 4, (c - NCTX) * P:(c - NCTX + 1) * P]
                        dve.tensor_tensor(h4(QE[q][:, :]), qs, h4(B[q][:, :]), ALU.mult).then_inc(qe_ready, 1)
                    for q in range(4):
                        need(qk_full)
                        dve.tensor_tensor(QKD[q][:, :], A[q][:, :], DEC[q][:, :], ALU.mult).then_inc(qkd_ready, 1)
                for q in range(4):
                    d, c = q // 2, GSEQ[q // 2][t]
                    need(ks_full)
                    for j in range(4):
                        h, s = 4 * (q % 2) + j, slice(j * P, (j + 1) * P)
                        o = dcol(d, c, SH + h)
                        ins = dve.scalar_tensor_tensor(out=RM[q][:, s], in0=B[q][:, s], scalar=neg_eg[:, o:o + 1],
                                                       in1=vt[:, c * D + h * P:c * D + (h + 1) * P], op0=ALU.mult, op1=ALU.add)
                    ins.then_inc(r_ready, 1)
                for q in range(4):
                    d, c = q // 2, GSEQ[q // 2][t]
                    if lat:
                        need(o_full)
                        if t == NCTX and q == 0:
                            need(y_spilled, 16)
                        dst = v3(ofm, GH)[:, 4 * (q % 2):4 * (q % 2) + 4, (c - NCTX) * P:(c - NCTX + 1) * P]
                        if t < NCTX + 2:
                            dve.tensor_copy(dst, h4(A[q][:, :])).then_inc(o_added, 1)
                        else:
                            dve.tensor_tensor(dst, dst, h4(A[q][:, :]), ALU.add).then_inc(o_added, 1)
                    if t < NCH - 1:
                        need(s_full)
                        for j in range(4):
                            s = slice(j * P, (j + 1) * P)
                            o = dcol(d, c, SH + 4 * (q % 2) + j)
                            ins = dve.scalar_tensor_tensor(out=S[q][:, s], in0=S[q][:, s], scalar=et[:, o:o + 1], in1=B[q][:, s],
                                                           op0=ALU.mult, op1=ALU.add)
                        ins.then_inc(s_ready, 1)
            barrier(dve, 4)

            g_n, t_n, sets = [0], [0], ["a"]
            two_pi = 2 * np.pi
            c1 = 6.28125
            c2 = float(np.float32(two_pi - c1))
            c3 = float(two_pi - c1 - np.float64(np.float32(two_pi - c1)))

            def next_rs():
                need(rs_ready)
                r = work[sets[0]][1][g_n[0] % 2]
                g_n[0] += 1
                return r[:, :]

            def split_tmp(items, rs_done=False):
                tps = work[sets[0]][2]
                n = len(items)
                for i in range(n + 1):
                    if i < n:
                        if t_n[0] >= 2:
                            dve.wait_ge(t_lo, t_n[0] - 1)
                        items[i][0](tps[t_n[0] % 2][:, :]).then_inc(t_ready, 1)
                        t_n[0] += 1
                    if i >= 1:
                        m = t_n[0] - (1 if i == n else 2)
                        _, hi, lo, bias = items[i - 1]
                        dve.wait_ge(t_hi, m + 1)
                        dve.wait_ge(t_ready, m + 1)
                        t = tps[m % 2][:, :]
                        if bias is None:
                            dve.tensor_tensor(lo, t, hi.bitcast(F32), ALU.subtract).then_inc(t_lo, 1)
                        else:
                            dve.scalar_tensor_tensor(out=lo, in0=t, scalar=bias, in1=hi.bitcast(F32), op0=ALU.add,
                                                     op1=ALU.subtract).then_inc(t_lo, 1)

            def free_rs():
                dve.wait_ge(t_ready, t_n[0])
                dve.nop().then_inc(rs_used, 1)

            def scaled_by(src, gain, r):
                return lambda t: dve.scalar_tensor_tensor(out=t, in0=src, scalar=gain, in1=r, op0=ALU.mult, op1=ALU.mult)

            need(tab_loaded, 32)
            after(dve.tensor_copy(rb[:, :], posb[:, :]))
            after(dve.tensor_scalar(rb[:, :], rb[:, :], vc("freq", 0, 1)[0:64], None, ALU.mult))
            after(dve.tensor_scalar(ra[:, :], rb[:, :], 1.0 / two_pi, None, ALU.mult))
            after(dve.tensor_copy(posb[:, :], ra[:, :]))
            after(dve.tensor_copy(ra[:, :], posb[:, :]))
            for cst in (c1, c2, c3):
                after(dve.scalar_tensor_tensor(out=rb[:, :], in0=ra[:, :], scalar=-cst, in1=rb[:, :], op0=ALU.mult, op1=ALU.add))
            after(dve.tensor_scalar(rb[:, :], rb[:, :], vc("freq", 1, 1)[0:64], None, ALU.add))
            after(dve.tensor_scalar(ra[:, :], rb[:, :], float(np.pi), -two_pi, ALU.is_gt, ALU.mult))
            after(dve.tensor_tensor(rb[:, :], rb[:, :], ra[:, :], ALU.add))
            after(dve.tensor_scalar(ra[:, :], rb[:, :], -float(np.pi), two_pi, ALU.is_lt, ALU.mult))
            after(dve.tensor_tensor(rb[:, :], rb[:, :], ra[:, :], ALU.add))
            dve.tensor_scalar(ra[:, :], rb[:, :], 3.1415925, -3.1415925, ALU.min, ALU.max).then_inc(rope_step, 1)
            need(back_loaded, 48)
            for b in range(KB):
                dve.tensor_tensor(blk(yb, b), blk(yb, b), blk(zb, b), ALU.mult).then_inc(v_ready, 1)
            for b in range(KB):
                dve.tensor_tensor(blk(gateb, b), blk(gateb, b), blk(ofm, b), ALU.mult).then_inc(v_ready, 1)
            need(len_rooted)
            dve.reciprocal(mn_rs[:, :], mn_root[:, :]).then_inc(len_inverse, 1)
            need(len_hi_ready)
            dve.wait_ge(len_inverse, 2)
            dve.tensor_tensor(mn_lo[:, :], mn_rs[:, :], mn_hi[:, :].bitcast(F32), ALU.subtract).then_inc(len_lo_ready, 1)

            def normed(i):
                g = i // 4 if i < KB else i - 6
                r = bank[4 + g % 2][:, :]

                def make(t):
                    if i >= KB or i % 4 == 0:
                        need(bc_full)
                    src, gain = (blk(yb, i), vc("ssdn", i, 1)) if i < KB else (blk(gateb, i - KB), vc("gdnn"))
                    return dve.scalar_tensor_tensor(out=t, in0=src, scalar=gain, in1=r, op0=ALU.mult, op1=ALU.mult)
                return make

            dve.wait_ge(v_ready, 2 * KB)
            split_tmp([(normed(i), blk(yhi, i), blk(ylo, i), None) for i in range(2 * KB)])
            need(rope_sin)
            after(dve.tensor_scalar(rope[0:64, :], rb[:, :], vc("freq", 2, 1)[0:64], None, ALU.mult))
            barrier(dve, 5)
            job = JOB["wout"]

            def residual(b, k, gain, done):
                if gain is None:
                    dve.tensor_tensor(blk(xr, b), bank[k][:, :], blk(xr, b), ALU.add).then_inc(out_taken, 1)
                else:
                    dve.scalar_tensor_tensor(out=blk(xr, b), in0=bank[k][:, :], scalar=gain, in1=blk(xr, b), op0=ALU.mult,
                                             op1=ALU.add).then_inc(out_taken, 1)

            def dve_wout(b, k, last):
                split_lo(dve, b * 2 + (job.u0 + 1), 1, KB)
                split_lo(dve, b * 2 + (job.u0 + 2), 0, KB)
                dve.wait_ge(unit_done, b * 2 + (job.u0 + 2))
                residual(b, k, pcol(aff, b + 24), None)

            need(xr_loaded, 16)
            in_turns(dve, need, job, {}, dve_wout)
            barrier(dve, 6)

            def dve_plain(job, evac=None):
                def body(b, k, last):
                    split_next(split_lo, dve, job, b, k, last)
                    if evac:
                        dve.wait_ge(unit_done, b + (job.u0 + 1))
                        evac(job, b, k)
                in_turns(dve, need, job, {}, body)

            def dve_up(job):
                def body(b, k, last):
                    split_next(split_lo, dve, job, b, k, last)
                    need(relu_ready)
                    t = work["b"][2][k][:, :]
                    dve.scalar_tensor_tensor(out=t, in0=bank[k][:, :], scalar=0.0, in1=rt[k][:, :], op0=ALU.max, op1=ALU.mult
                                             ).then_inc(t_ready, 1)
                    dve.wait_ge(t_ready, b + (t_n[0] + 1))
                    dve.nop().then_inc(out_taken, 1)
                    need(t_hi)
                    dve.tensor_tensor(blk(flo, b), t, blk(fhi, b).bitcast(F32), ALU.subtract).then_inc(t_lo, 1)
                in_turns(dve, need, job, {relu_ready: 2, t_hi: 2}, body)
                t_n[0] += job.n

            def norm_to_x(gain, bias=None):
                r = next_rs()
                split_tmp([(scaled_by(blk(xr, b), gain(b), r), blk(xhi, b), blk(xlo, b), bias and bias(b)) for b in range(KB)])
                free_rs()
                need.seen[t_hi.name] = t_n[0]

            sets[0] = "b"
            norm_to_x(lambda b: aff[:, 16 + b:17 + b], lambda b: aff[:, 32 + b:33 + b])
            for up, down in mlp_jobs():
                dve_up(up)
                dve_plain(down, lambda job, b, k: residual(b, k, pcol(aff, b + 40), None))
            barrier(dve, 7)
            r = next_rs()
            for b in range(KB):
                ins = dve.scalar_tensor_tensor(out=blk(xr, b), in0=blk(xr, b), scalar=vc("final1", b, 1), in1=r, op0=ALU.mult, op1=ALU.mult)
            ins.then_inc(rs_used, 1)
            barrier(dve, 8)
            for l in range(2):
                p0 = 8 + 4 * l
                norm_to_x(lambda b: vc(f"mixn{l}", b, 1))
                dve_plain(JOB[f"win{l}"])
                barrier(dve, p0 + 1)
                for n, base_, name in ((3, 0, "qn"), (2, 3, "kvn")):
                    r = next_rs()
                    split_tmp([(scaled_by(blk(pf, base_ + i), vc(f"{name}{l}", i, 1), r), blk(chi, base_ + i), blk(clo, base_ + i), None)
                               for i in range(n)])
                    free_rs()
                need(zero_ready)
                after(dve.tensor_tensor(rt[0][0:32, :], pf[32:64, 5 * LAT:6 * LAT], rope[32:64, :], ALU.mult))
                after(dve.tensor_tensor(rt[1][0:32, :], pf[0:32, 5 * LAT:6 * LAT], rope[0:32, :], ALU.mult))
                after(dve.tensor_tensor(kh[0:32, 0:LAT], rt[0][0:32, :], rt[1][0:32, :], ALU.add))
                after(dve.tensor_copy(kh[0:32, LAT:MH * LAT].rearrange("p (h t) -> p h t", h=MH - 1),
                                      kh[0:32, 0:LAT].unsqueeze(1).broadcast_to((32, MH - 1, LAT))))

                job = JOB[f"uq{l}"]

                def uq_body(b, k, last):
                    split_next(split_lo, dve, job, b, k, last)
                    dve.wait_ge(unit_done, b + (job.u0 + 1))
                    dve.scalar_tensor_tensor(out=rt[0][0:32, :], in0=bank[k][32:64, :], scalar=QS, in1=rope[32:64, :], op0=ALU.mult,
                                             op1=ALU.mult).then_inc(rope_step, 1)
                    dve.scalar_tensor_tensor(out=rt[1][0:32, :], in0=bank[k][0:32, :], scalar=QS, in1=rope[0:32, :], op0=ALU.mult,
                                             op1=ALU.mult).then_inc(rope_step, 1)
                    need(rope_step, 2)
                    dve.tensor_tensor(blk(qh, b)[0:32, :], rt[0][0:32, :], rt[1][0:32, :], ALU.add).then_inc(rope_ready, 1)
                    need(rope_ready)
                    need(act_part)
                    dve.nop().then_inc(out_taken, 1)

                need.seen[rope_step.name] = 1 + 16 * l
                in_turns(dve, need, job, {rope_step: 4, rope_ready: 2, act_part: 2}, uq_body)
                dve_plain(JOB[f"uk{l}"])
                job = JOB[f"uv{l}"]
                split_lo(dve, job.u0 + 1, 1, 4)
                split_lo(dve, job.u0 + 2, 0, job.next_kc)
                barrier(dve, p0 + 2)

                n_att = 4 * MH

                def maxima(m):
                    need(s2_full)
                    dve.tensor_reduce(smal[:, m % 3:m % 3 + 1], bank[(0, 1, 6)[m % 3]][:, :], AX.X, ALU.max, negate=True).then_inc(mx_ready, 1)

                maxima(0)
                maxima(1)
                for m in range(n_att):
                    need(e_ready)
                    after(dve.reciprocal(smal[:, 6 + m % 3:7 + m % 3], smal[:, 3 + m % 3:4 + m % 3]))
                    dve.tensor_scalar(eb[m % 3][:, :], eb[m % 3][:, :], smal[:, 6 + m % 3:7 + m % 3], None, ALU.mult).then_inc(pn_ready, 1)
                    if m + 2 < n_att:
                        maxima(m + 2)
                    if (m >= 4 and (m - 4) % 8 == 7) or m == n_att - 1:
                        hp = m // 8 - 1 if m < n_att - 1 else 3
                        need(ao_hi)
                        dve.tensor_tensor(blk(xlo, hp), bank[4 + hp % 2][:, :], blk(xhi, hp).bitcast(F32), ALU.subtract).then_inc(ao_taken, 1)
                for b in range(2):
                    need(pw_hi)
                    after(dve.scalar_tensor_tensor(out=blk(xlo, 4 + b), in0=bank[b][:, :], scalar=vc(f"psc{l}", b, 1),
                                                   in1=blk(xhi, 4 + b).bitcast(F32), op0=ALU.mult, op1=ALU.subtract))
                for b in range(2):
                    r = next_rs()
                    v = blk(pf, 10 + b)
                    dve.scalar_tensor_tensor(out=v, in0=v, scalar=vc(f"sgn{l}", b, 1), in1=r, op0=ALU.mult, op1=ALU.mult).then_inc(vn2_ready, 1)
                    dve.wait_ge(vn2_ready, 2 * l + b + 1)
                    dve.nop().then_inc(rs_used, 1)
                items = []
                for b in range(2):
                    def mixed(t, b=b):
                        need(sg_full)
                        after(dve.tensor_tensor(h4(t), h4(bank[4 + b][:, :]), b4(bsb[:, b * P:(b + 1) * P]), ALU.add))
                        return dve.tensor_tensor(t, t, blk(pf, 8 + b), ALU.mult)
                    items.append((mixed, blk(xhi, 6 + b), blk(xlo, 6 + b), None))
                split_tmp(items)
                barrier(dve, p0 + 3)
                dve_plain(JOB[f"wo{l}"], lambda job, b, k: residual(b, k, None, None))
                barrier(dve, p0 + 4)
                norm_to_x(lambda b: vc(f"ffn{l}", b, 1))

                def dve_gu(job):
                    def body(b, k, last):
                        split_next(split_lo, dve, job, b, k, last)
                        if k == 0:
                            return
                        dve.wait_ge(unit_done, b + (job.u0 + 1))
                        dve.wait_ge(out_taken, b + (job.b0 - JOB["zg"].b0))
                        t = work["b"][2][0][:, :]
                        dve.tensor_tensor(t, rt[0][:, :], bank[1][:, :], ALU.mult).then_inc(out_taken, 1)
                        dst, hi = ((blk(flo, b // 2), blk(fhi, b // 2)) if isinstance(b, int) else
                                   (flo[:, bass.ds(b * 256 - 256, LAT)], fhi[:, bass.ds(b * 256 - 256, LAT)]))
                        need(t_hi)
                        dve.nop().then_inc(t_ready, 1)
                        dve.tensor_tensor(dst, t, hi.bitcast(F32), ALU.subtract).then_inc(t_lo, 1)
                    in_turns(dve, need, job, {t_hi: 1}, body)
                    t_n[0] += job.n // 2

                for gu, dn in ffn_jobs(l):
                    dve_gu(gu)
                    dve_plain(dn, lambda job, b, k: residual(b, k, None, None))
            r = next_rs()
            for b in range(KB):
                dve.scalar_tensor_tensor(out=blk(xr, b), in0=blk(xr, b), scalar=vc("final2", b, 1), in1=r, op0=ALU.mult, op1=ALU.mult)
            barrier(dve, 17)

        @block.gpsimd
        def _(pool):
            need = Need(pool)
            for s in range(2):
                m = pool.memset(cbuf[s][:, :], 0.0)
            m.then_inc(pads_ready, 1)
            barrier(pool, 1)
            barrier(pool, 2)
            barrier(pool, 3)
            for t in range(NCH):
                for l in range(LEVELS):
                    for q in range(4):
                        if l == 0:
                            need(at_ready)
                        elif l == 1:
                            need(c1_full)
                            need(dt_ready)
                        else:
                            need(p_full)
                        pool.tensor_tensor(h4(CS[q][:, :]), h4(AT[q][:, :]), b4(cbf(3 + LEVELS * (q // 2) + l)), ALU.mult).then_inc(c_ready, 1)
                if t < NCH - 1:
                    need(p_full, 4)
                need.skip(dt_ready, 4 * (LEVELS - 1))
            barrier(pool, 4)
            barrier(pool, 5)
            barrier(pool, 6)
            barrier(pool, 7)
            barrier(pool, 8)
            for l in range(2):
                p0 = 8 + 4 * l
                barrier(pool, p0 + 1)
                for t in (qh, kh):
                    ins = pool.memset(t[32:64, :], 0.0)
                ins.then_inc(zero_ready, 1)
                barrier(pool, p0 + 2)
                need(tab_loaded, 32 + 48 if l == 0 else 48)
                n = [0]

                def then(ins):
                    ins.then_inc(pool_done, 1)
                    need(pool_done)

                x, y0, y1 = px[2], px[3], px[4]
                for t in (x, y0, y1):
                    then(pool.memset(t[:, :], 0.0))
                for b in range(2):
                    then(pool.tensor_copy(x[:, 8:8 + LAT], pf[:, (6 + b) * LAT:(7 + b) * LAT]))
                    levels = [(x, y0, 1, 527, 1, 0), (y0, y1, 2, 526, 1, 1), (y1, y0, 4, 524, 2, 2), (y0, y1, 8, 520, 4, 4)]
                    wide = {}
                    for i, (src, dst, lo, hi, back, ahead) in enumerate(levels[:2 + 2 * b]):
                        then(pool.tensor_tensor(dst[:, lo:hi], src[:, lo - back:hi - back], src[:, lo + ahead:hi + ahead], ALU.add))
                    halves = (y0, y1)
                    for e in range(2):
                        r = slice(64 * e, 64 * e + 64)
                        then(pool.tensor_tensor(px[b][r, 0:LAT], halves[e][r, 8:8 + LAT], cntb[r, b * LAT:(b + 1) * LAT], ALU.mult))
                    pool.tensor_tensor(px[b][:, 0:LAT], px[b][:, 0:LAT], x[:, 8:8 + LAT], ALU.subtract).then_inc(pd_ready, 1)
                    pool.wait_ge(pd_ready, 2 * l + b + 1)
                barrier(pool, p0 + 3)
                barrier(pool, p0 + 4)
            barrier(pool, 17)


_OUT = ((D, LAT), "float32")


def kernel(**inputs):
    import concourse.bacc as _bacc
    from concourse.bass_utils import run_bass_kernel_spmd as _run

    nc = _bacc.Bacc("TRN2", target_bir_lowering=False, num_devices=1)
    arrays = layout(**inputs)
    a = {n: nc.dram_tensor("in_" + n, v.shape, mybir.dt.from_np(v.dtype), kind="ExternalInput").ap() for n, v in arrays.items()}
    out = nc.dram_tensor("out_t", _OUT[0], F32, kind="ExternalOutput").ap()
    build_kernel(nc, a, out)
    r = _run(nc, [{"in_" + n: v for n, v in arrays.items()}], core_ids=[0])
    return np.ascontiguousarray(r.results[0]["out_t"].T)[None]
```
